# Optimizing a Trainium2 kernel written in Bass

```python
import math
import jax, jax.numpy as jnp
from jax import lax
import numpy as np

D_MODEL = 1024
BATCH = 1
SEQ = 1024
DEPTH = 1
DEC_BATCH = 1
DEC_SEQ = 32
PAST_LEN = 128

CHUNK = 64
D_MIX = D_MODEL
W_A = D_MIX // 2
W_B = D_MIX - W_A
LRU_BLOCKS = 8
LRU_BW = W_A // LRU_BLOCKS
CONV_W = 4
LRU_C = 8.0
H_B = 4
DK = W_B // H_B
DV = W_B // H_B
N_ADA = 6
PEER_HEADS = 8
N_KEYS = 128
N_EXPERTS = N_KEYS * N_KEYS
D_QUERY = 256
PEER_TOPK = 16
PEER_BLOCK = 128
EPS = 1e-6

OFF_XA = 0
OFF_GA = OFF_XA + W_A
OFF_Q = OFF_GA + W_A
OFF_K = OFF_Q + W_B
OFF_V = OFF_K + W_B
OFF_O = OFF_V + W_B
OFF_I = OFF_O + W_B
OFF_F = OFF_I + H_B
N_IN = OFF_F + H_B

kernel_name = 'hybrid_rglru_mlstm_peer_stream'

def rmsnorm(x, w):
    xf = x.astype(jnp.float32)
    y = xf * lax.rsqrt(jnp.mean(xf * xf, axis=-1, keepdims=True) + EPS)
    return (y * w.astype(jnp.float32)).astype(x.dtype)

def causal_conv(x, buf, w, b):
    T = x.shape[1]
    xp = jnp.concatenate([buf.astype(x.dtype), x], axis=1)
    y = b + xp[:, 0:T] * w[0]
    for k in range(1, CONV_W):
        y = y + xp[:, k:k + T] * w[k]
    return y, xp[:, xp.shape[1] - (CONV_W - 1):]

def _lin_combine(left, right):
    a_l, b_l = left
    a_r, b_r = right
    return a_l * a_r, a_r * b_l + b_r

def rglru(xa, ga, h0, conv0, conv_w, conv_b, wr, br, wi, bi, lam):
    B, T, _ = xa.shape
    u, conv_new = causal_conv(xa, conv0, conv_w, conv_b)
    uf = u.astype(jnp.float32)
    ub = uf.reshape(B, T, LRU_BLOCKS, LRU_BW)
    r = jax.nn.sigmoid(jnp.einsum('btnc,ncd->btnd', ub, wr.astype(jnp.float32)).reshape(B, T, W_A) + br)
    i = jax.nn.sigmoid(jnp.einsum('btnc,ncd->btnd', ub, wi.astype(jnp.float32)).reshape(B, T, W_A) + bi)
    log_a = -LRU_C * r * jax.nn.softplus(-lam.astype(jnp.float32))
    a = jnp.exp(log_a)
    bx = jnp.sqrt(-jnp.expm1(2.0 * log_a)) * (i * uf)
    a_cum, b_cum = lax.associative_scan(_lin_combine, (a, bx), axis=1)
    h = b_cum + a_cum * h0.astype(jnp.float32)[:, None, :]
    y = h * jax.nn.gelu(ga.astype(jnp.float32))
    return y.astype(xa.dtype), h[:, -1], conv_new

def mlstm_chunk(carry, inp):
    C, n, m = carry
    q, k, v, ig, lf = inp
    L = q.shape[2]
    b = jnp.cumsum(lf, axis=-1)
    causal = jnp.tril(jnp.ones((L, L), dtype=bool))
    logD = jnp.where(causal, b[..., :, None] - b[..., None, :] + ig[..., None, :], -jnp.inf)
    inter = b + m[..., None]
    m_t = jnp.maximum(inter, jnp.max(logD, axis=-1))
    D = jnp.exp(logD - m_t[..., None])
    w_state = jnp.exp(inter - m_t)
    S = jnp.einsum('bhtd,bhsd->bhts', q, k) * D
    num = jnp.einsum('bhts,bhse->bhte', S, v) + w_state[..., None] * jnp.einsum('bhtd,bhde->bhte', q, C)
    den = jnp.sum(S, axis=-1) + w_state * jnp.einsum('bhtd,bhd->bht', q, n)
    h = num / jnp.maximum(jnp.abs(den), jnp.exp(-m_t))[..., None]
    m_new = m_t[..., -1]
    w_k = jnp.exp(b[..., -1:] - b + ig - m_new[..., None])
    w_c = jnp.exp(inter[..., -1] - m_new)
    C_new = w_c[..., None, None] * C + jnp.einsum('bhs,bhsd,bhse->bhde', w_k, k, v)
    n_new = w_c[..., None] * n + jnp.einsum('bhs,bhsd->bhd', w_k, k)
    return (C_new, n_new, m_new), h

def mlstm(q, k, v, o, ig, fg, C0, n0, m0, norm_w, chunk_len):
    B, T, _ = q.shape

    def to_heads(t):
        return t.astype(jnp.float32).reshape(B, T, H_B, -1).transpose(0, 2, 1, 3)

    qh = to_heads(q) * (DK ** -0.5)
    kh = to_heads(k)
    vh = to_heads(v)
    igh = ig.astype(jnp.float32).transpose(0, 2, 1)
    lfh = jax.nn.log_sigmoid(fg.astype(jnp.float32)).transpose(0, 2, 1)
    nc = T // chunk_len

    def chunkify(t):
        return jnp.moveaxis(t.reshape((B, H_B, nc, chunk_len) + t.shape[3:]), 2, 0)

    carry0 = (C0.astype(jnp.float32), n0.astype(jnp.float32), m0.astype(jnp.float32))
    (C, n, m), hs = lax.scan(mlstm_chunk, carry0,
                             (chunkify(qh), chunkify(kh), chunkify(vh), chunkify(igh), chunkify(lfh)))
    h = jnp.moveaxis(hs, 0, 2).reshape(B, H_B, T, DV)
    h = h * lax.rsqrt(jnp.mean(h * h, axis=-1, keepdims=True) + EPS)
    h = h.transpose(0, 2, 1, 3).reshape(B, T, W_B) * norm_w.astype(jnp.float32)
    y = jax.nn.sigmoid(o.astype(jnp.float32)) * h
    return y.astype(q.dtype), C, n, m

def peer(h, wq, k1, k2, u, v):
    B, T, D = h.shape
    n_tok = B * T
    tok = h.reshape(n_tok, D)
    pad = (-n_tok) % PEER_BLOCK
    blocks = jnp.pad(tok, ((0, pad), (0, 0))).reshape(-1, PEER_BLOCK, D)

    def block_fn(xb):
        q = (xb @ wq).astype(jnp.float32).reshape(PEER_BLOCK, PEER_HEADS, D_QUERY)
        q = q * lax.rsqrt(jnp.mean(q * q, axis=-1, keepdims=True) + EPS)
        q1 = q[..., :D_QUERY // 2]
        q2 = q[..., D_QUERY // 2:]
        s1 = jnp.einsum('phd,kd->phk', q1, k1.astype(jnp.float32))
        s2 = jnp.einsum('phd,kd->phk', q2, k2.astype(jnp.float32))
        v1, i1 = lax.top_k(s1, PEER_TOPK)
        v2, i2 = lax.top_k(s2, PEER_TOPK)
        cand = (v1[..., :, None] + v2[..., None, :]).reshape(PEER_BLOCK, PEER_HEADS, PEER_TOPK * PEER_TOPK)
        sv, si = lax.top_k(cand, PEER_TOPK)
        e1 = jnp.take_along_axis(i1, si // PEER_TOPK, axis=-1)
        e2 = jnp.take_along_axis(i2, si % PEER_TOPK, axis=-1)
        expert = e1 * N_KEYS + e2
        g = jax.nn.softmax(sv, axis=-1)
        ue = jnp.take(u, expert, axis=0)
        act = jax.nn.gelu(jnp.einsum('phkd,pd->phk', ue, xb).astype(jnp.float32))
        ve = jnp.take(v, expert, axis=0)
        return jnp.einsum('phk,phkd->pd', (g * act).astype(xb.dtype), ve)

    out = lax.map(block_fn, blocks).reshape(-1, D)[:n_tok]
    return out.reshape(B, T, D)

def trunk_layer(x, c, h0, conv0, C0, n0, m0, chunk_len,
                norm1_w, ada_w, ada_b, w_in, b_in, conv_w, conv_b, lru_wr, lru_br, lru_wi, lru_bi,
                lru_lambda, mlstm_norm_w, w_out, norm2_w, peer_wq, peer_k1, peer_k2, peer_u, peer_v):
    B = x.shape[0]
    mod = (jax.nn.silu(c) @ ada_w + ada_b).reshape(B, N_ADA, 1, D_MODEL)
    sh1, sc1, g1, sh2, sc2, g2 = (mod[:, i] for i in range(N_ADA))
    h = rmsnorm(x, norm1_w) * (1.0 + sc1) + sh1
    z = h @ w_in + b_in
    ya, h_last, conv_new = rglru(z[..., OFF_XA:OFF_GA], z[..., OFF_GA:OFF_Q], h0, conv0,
                                 conv_w, conv_b, lru_wr, lru_br, lru_wi, lru_bi, lru_lambda)
    yb, C, n, m = mlstm(z[..., OFF_Q:OFF_K], z[..., OFF_K:OFF_V], z[..., OFF_V:OFF_O], z[..., OFF_O:OFF_I],
                        z[..., OFF_I:OFF_F], z[..., OFF_F:N_IN], C0, n0, m0, mlstm_norm_w, chunk_len)
    x = x + g1 * (jnp.concatenate([ya, yb], axis=-1) @ w_out)
    h2 = rmsnorm(x, norm2_w) * (1.0 + sc2) + sh2
    x = x + g2 * peer(h2, peer_wq, peer_k1, peer_k2, peer_u, peer_v)
    return x, h_last, conv_new, C, n, m

def setup_inputs(seed: int = 0) -> dict:
    key = jax.random.key(seed)
    ks = jax.random.split(key, 32)
    f32 = jnp.float32

    def nrm(k, shape, s):
        return s * jax.random.normal(k, shape, f32)

    a_c = jax.random.uniform(ks[21], (DEPTH, W_A), f32, 0.9, 0.999)
    sig = a_c ** (1.0 / LRU_C)
    b_in = nrm(ks[13], (DEPTH, N_IN), 0.01).at[:, OFF_F:OFF_F + H_B].add(
        jax.random.uniform(ks[14], (DEPTH, H_B), f32, 3.0, 6.0))
    return {
        'x_prompt': nrm(ks[0], (BATCH, SEQ, D_MODEL), 1.0),
        'x_sample': nrm(ks[1], (DEC_BATCH, DEC_SEQ, D_MODEL), 1.0),
        'c_prompt': nrm(ks[2], (BATCH, D_MODEL), 1.0),
        'c_sample': nrm(ks[3], (DEC_BATCH, D_MODEL), 1.0),
        'state_lru_h': nrm(ks[4], (DEPTH, DEC_BATCH, W_A), 0.5),
        'state_lru_conv': nrm(ks[5], (DEPTH, DEC_BATCH, CONV_W - 1, W_A), 1.0),
        'state_mlstm_C': nrm(ks[6], (DEPTH, DEC_BATCH, H_B, DK, DV), 0.1),
        'state_mlstm_n': nrm(ks[7], (DEPTH, DEC_BATCH, H_B, DK), 0.5),
        'state_mlstm_m': nrm(ks[8], (DEPTH, DEC_BATCH, H_B), 1.0),
        'norm1_w': 1.0 + nrm(ks[9], (DEPTH, D_MODEL), 0.01),
        'ada_w': nrm(ks[10], (DEPTH, D_MODEL, N_ADA * D_MODEL), 0.5 * D_MODEL ** -0.5),
        'ada_b': nrm(ks[11], (DEPTH, N_ADA * D_MODEL), 0.01),
        'w_in': nrm(ks[12], (DEPTH, D_MODEL, N_IN), D_MODEL ** -0.5),
        'b_in': b_in,
        'conv_w': nrm(ks[15], (DEPTH, CONV_W, W_A), CONV_W ** -0.5),
        'conv_b': nrm(ks[16], (DEPTH, W_A), 0.01),
        'lru_wr': nrm(ks[17], (DEPTH, LRU_BLOCKS, LRU_BW, LRU_BW), LRU_BW ** -0.5),
        'lru_br': nrm(ks[18], (DEPTH, W_A), 0.01),
        'lru_wi': nrm(ks[19], (DEPTH, LRU_BLOCKS, LRU_BW, LRU_BW), LRU_BW ** -0.5),
        'lru_bi': nrm(ks[20], (DEPTH, W_A), 0.01),
        'lru_lambda': jnp.log(sig) - jnp.log1p(-sig),
        'mlstm_norm_w': 1.0 + nrm(ks[22], (DEPTH, W_B), 0.01),
        'w_out': nrm(ks[23], (DEPTH, D_MIX, D_MODEL), D_MIX ** -0.5),
        'norm2_w': 1.0 + nrm(ks[24], (DEPTH, D_MODEL), 0.01),
        'peer_wq': nrm(ks[25], (DEPTH, D_MODEL, PEER_HEADS * D_QUERY), D_MODEL ** -0.5),
        'peer_k1': nrm(ks[26], (DEPTH, N_KEYS, D_QUERY // 2), (D_QUERY // 2) ** -0.5),
        'peer_k2': nrm(ks[27], (DEPTH, N_KEYS, D_QUERY // 2), (D_QUERY // 2) ** -0.5),
        'peer_u': nrm(ks[28], (DEPTH, N_EXPERTS, D_MODEL), D_MODEL ** -0.5),
        'peer_v': nrm(ks[29], (DEPTH, N_EXPERTS, D_MODEL), 1.0),
        'final_norm_w': 1.0 + nrm(ks[30], (D_MODEL,), 0.01),
    }

def reference(x_prompt, x_sample, c_prompt, c_sample, state_lru_h, state_lru_conv, state_mlstm_C,
              state_mlstm_n, state_mlstm_m, norm1_w, ada_w, ada_b, w_in, b_in, conv_w, conv_b,
              lru_wr, lru_br, lru_wi, lru_bi, lru_lambda, mlstm_norm_w, w_out, norm2_w,
              peer_wq, peer_k1, peer_k2, peer_u, peer_v, final_norm_w):
    B = x_prompt.shape[0]
    dt = x_prompt.dtype
    xp = x_prompt
    xs = x_sample
    new_p = [[], [], [], [], []]
    new_s = [[], [], [], [], []]
    for l in range(DEPTH):
        w_l = (norm1_w[l], ada_w[l], ada_b[l], w_in[l], b_in[l], conv_w[l], conv_b[l],
               lru_wr[l], lru_br[l], lru_wi[l], lru_bi[l], lru_lambda[l], mlstm_norm_w[l],
               w_out[l], norm2_w[l], peer_wq[l], peer_k1[l], peer_k2[l], peer_u[l], peer_v[l])
        xp, *st_p = trunk_layer(xp, c_prompt,
                                jnp.zeros((B, W_A), dt), jnp.zeros((B, CONV_W - 1, W_A), dt),
                                jnp.zeros((B, H_B, DK, DV), dt), jnp.zeros((B, H_B, DK), dt),
                                jnp.zeros((B, H_B), dt), CHUNK, *w_l)
        xs, *st_s = trunk_layer(xs, c_sample, state_lru_h[l], state_lru_conv[l], state_mlstm_C[l],
                                state_mlstm_n[l], state_mlstm_m[l], xs.shape[1], *w_l)
        for j in range(5):
            new_p[j].append(st_p[j])
            new_s[j].append(st_s[j])
    y_prompt = rmsnorm(xp, final_norm_w)
    y_sample = rmsnorm(xs, final_norm_w)
    p_h = jnp.stack(new_p[0]).astype(state_lru_h.dtype)
    p_conv = jnp.stack(new_p[1]).astype(state_lru_conv.dtype)
    p_C = jnp.stack(new_p[2]).astype(state_mlstm_C.dtype)
    p_n = jnp.stack(new_p[3]).astype(state_mlstm_n.dtype)
    p_m = jnp.stack(new_p[4]).astype(state_mlstm_m.dtype)
    s_h = jnp.stack(new_s[0]).astype(state_lru_h.dtype)
    s_conv = jnp.stack(new_s[1]).astype(state_lru_conv.dtype)
    s_C = jnp.stack(new_s[2]).astype(state_mlstm_C.dtype)
    s_n = jnp.stack(new_s[3]).astype(state_mlstm_n.dtype)
    s_m = jnp.stack(new_s[4]).astype(state_mlstm_m.dtype)
    return (y_prompt, y_sample, p_h, p_conv, p_C, p_n, p_m, s_h, s_conv, s_C, s_n, s_m)


_drawn_inputs = setup_inputs


def setup_inputs(seed=0):
    import zlib

    import numpy as np

    out = dict(_drawn_inputs(seed))
    spreads = {}
    factors = {'state_mlstm_C': 5.882,
     'state_mlstm_n': 25.84,
     'state_mlstm_m': 5.515,
     'norm1_w': 2.934,
     'lru_br': 8.0,
     'lru_bi': 8.0,
     'mlstm_norm_w': 7.747,
     'norm2_w': 2.894,
     'final_norm_w': 29.862}
    for name, (base, spread) in spreads.items():
        noise = np.random.default_rng([zlib.crc32(name.encode()), seed]).standard_normal(out[name].shape)
        drawn = base * np.exp(spread * noise) if base else spread * noise
        out[name] = __import__('jax').numpy.asarray(drawn.astype(out[name].dtype))
    for name, factor in factors.items():
        out[name] = (out[name] * factor).astype(out[name].dtype)
    return out
```

```python
from contextlib import ExitStack

import concourse.bass as bass
from concourse import mybir

F32 = mybir.dt.float32
BF16 = mybir.dt.bfloat16
I32 = mybir.dt.int32
U32 = mybir.dt.uint32
ALU = mybir.AluOpType
ACT = mybir.ActivationFunctionType
AXX = mybir.AxisListType.X

P = 128
D = 1024
KD = D // P
SEQ, DEC = 1024, 32
T = SEQ + DEC
NT = SEQ // P + 1
W_A = W_B = 512
FT = W_A // P
CONV_W = 4
PAD = CONV_W - 1
LRU_C = 8.0
H_B = 4
DK = P
N_IN = 2 * W_A + 4 * W_B + 2 * H_B
HEADS, TOPK = 8, 16
DQ = 256
EPS = 1e-6
ZG = T // 3
XL = PAD + SEQ + PAD + DEC
UL = XL - PAD
LG = UL // 3
NEG = -1.0e30
NEG_MAX = -3.0e38
K_ROUTE, K_MIX, K_FIN = 14, 6, 2
EXP_MAX = 80.0
GELU_C = 0.044715
GELU_S = 2.0 * 0.7978845608028654
LOG1P = [1.0 / k for k in range(3, 19, 2)]

OUTS = [(1, SEQ, D), (1, DEC, D), (1, 1, W_A), (1, 1, PAD, W_A), (1, 1, H_B, DK, DK), (1, 1, H_B, DK),
        (1, 1, H_B), (1, 1, W_A), (1, 1, PAD, W_A), (1, 1, H_B, DK, DK), (1, 1, H_B, DK), (1, 1, H_B)]


def rows(t):
    return P if t < NT - 1 else DEC


def stream(t):
    return 0 if t < NT - 1 else 1


def build(nc, A, outs):
    with ExitStack() as ctx:
        def sb(name, shape, dt=F32):
            return ctx.enter_context(nc.sbuf_tensor(name, shape, dt))

        def sem(name):
            return ctx.enter_context(nc.semaphore(name))

        mod_dram = nc.dram_tensor("mod_dram", (2, 6 * D), F32, kind="Internal").ap()
        x1_dram = nc.dram_tensor("x1_dram", (T, D), F32, kind="Internal").ap()

        r_hT = sb("r_hT", [P, KD * T])
        r_qk = sb("r_qk", [P, NT * D])
        r_vo = sb("r_vo", [P, NT * (4 * 129 + 512)])
        r_yT = sb("r_yT", [P, KD * T])
        r_w = sb("r_w", [P, 12288])
        r_wq = sb("r_wq", [P, 4 * 516])
        ident = sb("ident", [P, P])
        ones = sb("ones", [P, P])
        mask = sb("mask", [P, P])
        seleye = sb("seleye", [H_B, H_B, P])
        wrd = sb("wrd", [P, FT, P])
        wid = sb("wid", [P, FT, P])
        kTt = sb("kTt", [P, 2, P])
        pos16 = sb("pos16", [P, TOPK])
        prm = sb("prm", [P, 520])
        gidx = sb("gidx", [P, NT * TOPK], I32)
        gate = sb("gate", [P, NT * TOPK])

        hT = r_hT[:, :].rearrange("p (k t) -> p k t", k=KD)
        xin = r_vo[:, 0:NT * D].rearrange("p (t d) -> p t d", t=NT)
        ada = r_w[:, :].rearrange("p (s k n) -> p s k n", s=3, k=KD)
        abias = r_yT[0:1, 0:1536].rearrange("p (s n) -> p s n", s=3)
        modrow = r_yT[0:2, 1536:2560].rearrange("p (s n) -> p s n", s=2)
        sq_junk = r_yT[:, 2560:3584]
        wblk = r_w[:, :].rearrange("p (s k n) -> p s k n", s=12, k=KD)
        qT = r_qk[:, 0:4 * T].rearrange("p (h t) -> p h t", h=H_B)
        kT = r_qk[:, 4 * T:8 * T].rearrange("p (h t) -> p h t", h=H_B)
        yT = r_yT[:, :].rearrange("p (k t) -> p k t", k=KD)
        lru = [r_vo[:, i * XL:(i + 1) * XL] for i in range(8)] + [r_yT[:, 4 * T + i * XL:4 * T + (i + 1) * XL] for i in range(3)]
        xpad, ga, uu = lru[0:2], lru[2:4], lru[4:6]
        rr, ii, aa, dd, pp = lru[6], lru[7], lru[8], lru[9], lru[10]
        wv = r_w[:, 4096:8192].rearrange("p (k n) -> p k n", k=KD)
        wo = r_w[:, 8192:12288].rearrange("p (k n) -> p k n", k=KD)
        vext = r_vo[:, 0:NT * 516].rearrange("p (t h e) -> p t h e", t=NT, h=H_B)
        og = r_vo[:, NT * 516:NT * 1028].rearrange("p (t n) -> p t n", t=NT)
        ra = [r_yT[0:8, (4 + i) * T:(5 + i) * T] for i in range(4)]
        zif, fro, aro, mro = ra[0], ra[1][0:H_B], ra[2][0:H_B], ra[3][0:H_B]
        negm = ra[1][0:H_B, 0:1024].rearrange("p (s h t) -> p s h t", s=2, h=H_B)
        wst, nmr, wkr = (r_w[0:H_B, i * T:(i + 1) * T] for i in range(3))
        hh = r_hT[:, 0:NT * 512].rearrange("p (t n) -> p t n", t=NT)
        o0 = NT * 512
        decay = [r_hT[:, o0 + i * 512:o0 + (i + 1) * 512].rearrange("p (h t) -> p h t", h=H_B) for i in range(2)]
        prob = [r_hT[:, o0 + 1024 + i * 512:o0 + 1536 + i * 512].rearrange("p (h t) -> p h t", h=H_B) for i in range(2)]
        kw = r_hT[:, o0 + 2048:o0 + 2560].rearrange("p (h t) -> p h t", h=H_B)
        nd = [r_hT[:, o0 + 2560 + i * 516:o0 + 3076 + i * 516].rearrange("p (h e) -> p h e", h=H_B) for i in range(2)]
        cst = r_wq[:, :].rearrange("p (b h e) -> p b h e", b=4, h=H_B)
        wout = r_w[:, 4096:12288].rearrange("p (k n) -> p k n", k=KD)
        xr = r_w[:, 0:4096].rearrange("p (s d) -> p s d", s=4)
        g1b, sh2b, a2b = (r_vo[:, i * 2048:(i + 1) * 2048].rearrange("p (s d) -> p s d", s=2) for i in range(3))
        n2b = r_vo[:, 6144:7168]
        h2 = r_qk[:, :].rearrange("p (t d) -> p t d", t=NT)
        h2T = hT
        wqh = r_wq[:, 0:2048].rearrange("p (k n) -> p k n", k=KD)
        uring = r_yT[:, 0:8192].rearrange("p (s d) -> p s d", s=8)
        vring = r_w[:, 4096:12288].rearrange("p (s d) -> p s d", s=8)
        acc = r_vo[:, 0:NT * D].rearrange("p (t d) -> p t d", t=NT)
        bt = r_w[:, 0:4096]
        bat = [0]

        def work(n):
            bat[0] += n
            return bt[:, bat[0] - n:bat[0]]

        diag = work(512).rearrange("p (s d) -> p s d", s=4)
        qts = work(256).rearrange("p (c t) -> p c t", c=2)
        qsq = work(256).rearrange("p (c t) -> p c t", c=2)
        swk, cand, cand2 = work(256), work(256), work(256)
        hot = [work(256).rearrange("p (a b) -> p a b", a=TOPK) for _ in range(2)]
        udump = [work(512).bitcast(BF16) for _ in range(2)]
        top, topf, sabf, e12 = work(32), work(32), work(32), work(32)
        topi, sab = work(32).bitcast(U32), work(32).bitcast(U32)
        sv, si = work(16), work(16).bitcast(U32)
        pexp, dots, gl, gl2, wgt = (work(TOPK) for _ in range(5))
        uidx, vidx = work(TOPK).bitcast(I32), work(TOPK).bitcast(I32)
        qrt, qrs, nsv0, psm, prs, fss, frs = (work(1) for _ in range(7))
        gidx_t = gidx[:, :].rearrange("p (t j) -> p t j", t=NT)
        gate_t = gate[:, :].rearrange("p (t j) -> p t j", t=NT)
        h2T_t = h2T[:, :, 0:SEQ].rearrange("p k (t c) -> p k t c", c=P)
        g2b = r_hT[:, 0:2048].rearrange("p (s d) -> p s d", s=2)
        fwb = r_hT[:, 2048:3072]
        x1s, ys, fdump = (r_hT[:, 3072 + i * D:4096 + i * D] for i in range(3))

        at = [0]

        def col(n):
            at[0] += n
            return prm[:, at[0] - n:at[0]]

        cT = col(16).rearrange("p (s k) -> p s k", s=2)
        ce = col(16).rearrange("p (s k) -> p s k", s=2)
        csil = col(16).rearrange("p (s k) -> p s k", s=2)
        n1T = col(8)
        modT = col(32).rearrange("p (a s k) -> p a s k", a=2, s=2)
        mul1 = col(16).rearrange("p (s k) -> p s k", s=2)
        binT = col(16)
        binq = col(4)
        bif = col(1)
        convw = col(16).rearrange("p (k f) -> p k f", k=CONV_W)
        convb, nbr, nbi, lam, lt1, lt2, c8, nc8 = (col(4) for _ in range(8))
        h0T = col(4)
        cv0 = col(12).rearrange("p (f r) -> p f r", f=FT)
        hl = col(8).rearrange("p (s f) -> p s f", s=2)
        cvn = col(24).rearrange("p (s f r) -> p s f r", s=2, f=FT)
        wif = col(64).rearrange("p (k n) -> p k n", k=KD)
        ssq = col(NT)
        rstd1 = col(NT)
        ssqh = col(36)
        rsth = col(36)
        mprev = col(NT)
        mend = col(2)
        mlast = col(NT)
        wcr = col(NT)
        wcd = col(36).rearrange("p (c h) -> p c h", c=NT)
        wcb = col(36).rearrange("p (c h) -> p c h", c=NT)
        den = col(4)
        rden = col(4)
        epsc = col(1)
        ssq2 = col(NT)
        rstd2 = col(NT)
        assert at[0] <= 520, at[0]
        ra2 = sb("colsx", [P, NT * 12])
        colT = ra2[:, :].rearrange("p (t a h) -> p t a h", t=NT, a=3)
        nwb = r_qk[:, 8 * T:8 * T + W_B]
        bvo = [wrd[0:1, :, :].rearrange("p f n -> p (f n)"), wid[0:1, :, :].rearrange("p f n -> p (f n)")]
        kts = r_yT[:, 3584:3840]
        kwj = r_hT[:, 8200:8328]
        sq2 = r_vo[:, 7168:8192]

        ps = ctx.enter_context(nc.psum_tensor("ps", [P, 8, 512], F32))

        ld_c, ld_prm, ld_x, ld_modT = sem("ld_c"), sem("ld_prm"), sem("ld_x"), sem("ld_modT")
        ada_ld = [sem(f"ada_ld{i}") for i in range(3)]
        ada_mm, mod_ev = sem("ada_mm"), sem("mod_ev")
        mod_st = [sem(f"mod_st{i}") for i in range(2)]
        c_exp, c_silu = sem("c_exp"), sem("c_silu")
        consts, x_sq, x_rt, x_sc, x_tr, x_evd, x_eva, mul1_ready = (sem(n) for n in (
            "consts", "x_sq", "x_rt", "x_sc", "x_tr", "x_evd", "x_eva", "mul1_ready"))
        w_ld = [sem(f"w_ld{i}") for i in range(12)]
        vo_ld, wout_ld = [sem("v_ld"), sem("o_ld")], sem("wout_ld")
        z_mm, z_ev, lg_mm, lg_ev = (sem(n) for n in ("z_mm", "z_ev", "lg_mm", "lg_ev"))
        conv_done, rg_ready, lru_ac, lru_d3, lru_d4a, lru_bx, lru_scan, lru_y = (sem(n) for n in (
            "conv_done", "rg_ready", "lru_ac", "lru_d3", "lru_d4a", "lru_bx", "lru_scan", "lru_y"))
        lam_abs, lam_exp, c8_ready = sem("lam_abs"), sem("lam_exp"), sem("c8_ready")
        f_ld, f_abs, f_exp, row_ready, row_exp, row_tr, col_ready = (sem(n) for n in (
            "f_ld", "f_abs", "f_exp", "row_ready", "row_exp", "row_tr", "col_ready"))
        v_ones, og_ready = sem("v_ones"), sem("og_ready")
        st_ld = sem("st_ld")
        negm_ready, k_tr, kw_ready, s_mm, d_mm, d_exp, p_ready, c_mm, c_upd, n_mm, i_mm, n_ev, nd_done, h_ready, h_sq = (
            sem(n) for n in ("negm_ready", "k_tr", "kw_ready", "s_mm", "d_mm", "d_exp", "p_ready", "c_mm", "c_upd",
                             "n_mm", "i_mm", "n_ev", "nd_done", "h_ready", "h_sq"))
        h_rt, y_ready, y_tr, y_ev = sem("h_rt"), sem("y_ready"), sem("y_tr"), sem("y_ev")
        bc_ld, a2_ready = sem("bc_ld"), sem("a2_ready")
        xr_ld = [sem(f"xr_ld{i}") for i in range(4)]
        x1_st = [sem(f"x1_st{i}") for i in range(4)]
        o_mm, x1_ready, x1_sq, x1_rt, h2_ready, h2_tr, h2_ev = (sem(n) for n in (
            "o_mm", "x1_ready", "x1_sq", "x1_rt", "h2_ready", "h2_tr", "h2_ev"))
        kt_ld, kt_tr, kt_ready = sem("kt_ld"), sem("kt_tr"), sem("kt_ready")
        dve_step, act_step, pool_step = sem("dve_step"), sem("act_step"), sem("pool_step")
        out_st, bvo_ld = sem("out_st"), sem("bvo_ld")
        wq_ld, q_mm, q_sb, q_rt, r_mm, r_cp, p_in, p_exp, idx_ready, idx_cp = (sem(n) for n in (
            "wq_ld", "q_mm", "q_sb", "q_rt", "r_mm", "r_cp", "p_in", "p_exp", "idx_ready", "idx_cp"))
        u_ld = [sem(f"u_ld{j}") for j in range(8)]
        v_ld = [sem(f"v_ld{j}") for j in range(8)]
        u_free, v_free, g_in, g_exp, w_ready, dg_ready, acc_done = (sem(n) for n in (
            "u_free", "v_free", "g_in", "g_exp", "w_ready", "dg_ready", "acc_done"))
        route_step, mix_step, fin_step = sem("route_step"), sem("mix_step"), sem("fin_step")
        g2_ld, x1_ld, f_sq, f_var, f_rt, y_out, y_st = (sem(n) for n in (
            "g2_ld", "x1_ld", "f_sq", "f_var", "f_rt", "y_out", "y_st"))
        pool_turn, pe_turn, act_turn, dve_turn = sem("pool_turn"), sem("pe_turn"), sem("act_turn"), sem("dve_turn")
        LAST = HEADS - 1
        N_STATE_STORES = 2 * (1 + FT + 1 + 2)
        n_out, n_prm = [0], [0]

        class Chain:

            def __init__(self, eng, s):
                self.eng, self.s, self.n, self.base = eng, s, 0, 0

            def link(self, ins):
                self.n += 1
                ins.then_inc(self.s, 1)
                self.eng.wait_ge(self.s, self.base + self.n)

        def heads_and_tiles(eng, step, last_step):
            with eng.Fori(0, LAST) as h:
                with eng.Fori(0, NT - 1) as t:
                    step(h, t, h * NT + t, P)
                step(h, NT - 1, h * NT + (NT - 1), DEC)
            with eng.Fori(0, NT - 1) as t:
                last_step(LAST, t, t + LAST * NT, P)
            last_step(LAST, NT - 1, NT - 1 + LAST * NT, DEC)

        block = ctx.enter_context(nc.Block())

        lb = ["xa0", "ga0", "xa1", "G0", "ga1", "xa2", "G1", "ga2", "xa3", "G2", "ga3", "q0", "G3", "q1", "q2", "q3",
              "k0", "k1", "k2", "k3"]
        zblocks = [b for b in lb if b[0] != "G"]
        zcol = {"xa": 0, "ga": 4, "q": 8, "k": 12}

        def blk(b):
            return b[:-1], int(b[-1]), (zcol[b[:-1]] + int(b[-1]))

        def col_view(a, n):
            return a.rearrange("(j p) -> p j", p=P)

        @block.sync
        def _(sp):
            sp.dma_start(cT[:, 0, :], A["c_prompt"].rearrange("a (k p) -> p (a k)", p=P),
                         allow_slow_non_contiguous=True).then_inc(ld_c, 16)
            sp.dma_start(cT[:, 1, :], A["c_sample"].rearrange("a (k p) -> p (a k)", p=P),
                         allow_slow_non_contiguous=True).then_inc(ld_c, 16)
            ada_v = A["ada_w"][0].rearrange("(k p) n -> p k n", p=P)
            for b in range(12):
                if b >= 3:
                    sp.wait_ge(ada_mm, b - 2)
                sp.dma_start(ada[:, b % 3], ada_v[:, :, b * 512:(b + 1) * 512]).then_inc(ada_ld[b % 3], 16)
                sp.dma_start(abias[:, b % 3, :], A["ada_b"][:, b * 512:(b + 1) * 512]).then_inc(ada_ld[b % 3], 16)
            win_v = A["w_in"][0].rearrange("(k p) n -> p k n", p=P)
            for i, b in enumerate(zblocks):
                if i < 12:
                    sp.wait_ge(ada_mm, 10 + i // 4)
                else:
                    sp.wait_ge(z_mm, 3 * (i - 11))
                c = blk(b)[2] * P
                sp.dma_start(wblk[:, i % 12], win_v[:, :, c:c + P]).then_inc(w_ld[i % 12], 16)
            for n, dst in enumerate((wv, wo)):
                sp.wait_ge(z_mm, 3 * (8 + 4 * n))
                c = 2 * W_A + (2 + n) * W_B
                sp.dma_start(dst, win_v[:, :, c:c + W_B]).then_inc(vo_ld[n], 16)
            sp.wait_ge(z_mm, 51 + 2 * NT)
            sp.dma_start(wout, A["w_out"][0].rearrange("(k p) n -> p k n", p=P)).then_inc(wout_ld, 16)
            sp.wait_ge(col_ready, 2)
            xs = [A["x_prompt"][0, t * P:(t + 1) * P, :] for t in range(NT - 1)] + [A["x_sample"][0]]
            for t in range(NT):
                if t >= 4:
                    sp.wait_ge(x1_st[t % 4], 16 * (t // 4))
                    sp.wait_ge(x1_sq, t - 3)
                    sp.wait_ge(h2_ready, t - 3)
                sp.dma_start(xr[0:rows(t), t % 4, :], xs[t]).then_inc(xr_ld[t % 4], 16)
            wq_v = A["peer_wq"][0].rearrange("(k p) (h n) -> p k h n", p=P, h=HEADS)
            sp.wait_ge(i_mm, NT)
            sp.wait_ge(out_st, 16 * N_STATE_STORES)
            sp.dma_start(wqh, wq_v[:, :, 0, :]).then_inc(wq_ld, 16)
            with sp.Fori(1, HEADS) as h:
                sp.wait_ge(q_mm, h * NT)
                sp.dma_start(wqh, wq_v[:, :, h, :]).then_inc(wq_ld, 16)
            sp.wait_ge(q_mm, HEADS * NT)
            for s in range(2):
                n = P if s == 0 else DEC
                sp.dma_start(g2b[0:n, s, :], mod_dram[s, 5 * D:6 * D].partition_broadcast(n)).then_inc(g2_ld, 16)
            sp.dma_start(fwb, A["final_norm_w"].partition_broadcast(P)).then_inc(g2_ld, 16)
            for s in range(4):
                sp.wait_ge(x1_st[s], 16 * (3 if s == 0 else 2))
            x1_t = x1_dram[0:SEQ].rearrange("(t p) d -> t p d", p=P)
            y_t = outs[0][0].rearrange("(t p) d -> t p d", p=P)

            def finish(t, r, src, dst):
                sp.dma_start(x1s[0:r], src).then_inc(x1_ld, 16)
                sp.wait_ge(y_out, t + 1)
                sp.dma_start(dst, ys[0:r]).then_inc(y_st, 16)

            sp.sem_inc(y_st, 16)
            with sp.Fori(0, NT - 1) as t:
                finish(t, P, x1_t[t], y_t[t])
            finish(NT - 1, DEC, x1_dram[SEQ:T], outs[1][0])
            sp.wait_ge(y_st, 16 * NT + 16)

        @block.gpsimd
        def _(pool):
            ch = Chain(pool, pool_step)
            for m, v in ((ident[:, :], 0.0), (mask[:, :], 0.0), (seleye[:, :, :], 0.0), (wrd[:, :, :], 0.0),
                         (wid[:, :, :], 0.0), (ones[:, :], 1.0), (ssq, 1.0), (ssqh, 1.0), (ssq2, 1.0)):
                ch.link(nc.gpsimd.memset(m, v))
            ch.link(nc.gpsimd.affine_select(out=ident[:, :], in_=ident[:, :], compare_op=ALU.not_equal, fill=1.0, base=0,
                                            pattern=[[-1, P]], channel_multiplier=1))
            ch.link(nc.gpsimd.affine_select(out=mask[:, :], in_=mask[:, :], compare_op=ALU.is_ge, fill=NEG, base=0,
                                            pattern=[[1, P]], channel_multiplier=-1))
            ch.link(nc.gpsimd.affine_select(out=seleye[:, :, :], in_=seleye[:, :, :], compare_op=ALU.not_equal, fill=1.0,
                                            base=0, pattern=[[-1, H_B], [0, P]], channel_multiplier=1))
            nc.gpsimd.iota(pos16[:, :], pattern=[[1, TOPK]], base=0, channel_multiplier=0,
                           allow_small_or_imprecise_dtypes=True).then_inc(consts, 1)

            def load(dst, src):
                n_prm[0] += 16
                pool.dma_start(dst, src, allow_slow_non_contiguous=True).then_inc(ld_prm, 16)

            load(n1T, col_view(A["norm1_w"][0], 8))
            load(binT, col_view(A["b_in"][0, 0:2048], 16))
            load(bif[0:8], A["b_in"][0, 3072:3080].rearrange("(p j) -> p j", j=1))
            load(convw, A["conv_w"][0].rearrange("k (f p) -> p k f", p=P))
            for dst, nm in ((convb, "conv_b"), (nbr, "lru_br"), (nbi, "lru_bi"), (lam, "lru_lambda")):
                load(dst, col_view(A[nm][0], 4))
            load(h0T, col_view(A["state_lru_h"][0, 0], 4))
            for f in range(FT):
                load(cv0[:, f, :], A["state_lru_conv"][0, 0, :, f * P:(f + 1) * P].rearrange("r p -> p r"))
            for half in range(2):
                hs = slice(64 * half, 64 * half + 64)
                load(wrd[hs, :, hs], A["lru_wr"][0, half::2].rearrange("n c d -> c n d"))
                load(wid[hs, :, hs], A["lru_wi"][0, half::2].rearrange("n c d -> c n d"))
            load(wif, A["w_in"][0, :, 3072:3080].rearrange("(k p) n -> p k n", p=P))
            load(nwb[:, :], A["mlstm_norm_w"][0].partition_broadcast(P))
            load(mprev[0:H_B, NT - 1:NT], A["state_mlstm_m"][0, 0].rearrange("(p j) -> p j", j=1))
            for b in range(12):
                pool.wait_ge(mod_ev, b + 1)
                pool.dma_start(mod_dram[:, b * 512:(b + 1) * 512], modrow[:, b % 2, :]).then_inc(mod_st[b % 2], 16)
                if b == 3:
                    for s in range(2):
                        pool.wait_ge(mod_st[s], 32)
                    for a in range(2):
                        for s in range(2):
                            pool.dma_start(modT[:, a, s, :], col_view(mod_dram[s, a * D:(a + 1) * D], 8),
                                           allow_slow_non_contiguous=True).then_inc(ld_modT, 16)
            for s in range(2):
                pool.wait_ge(mod_st[s], 96)
            pool.wait_ge(z_ev, 51)
            pool.dma_start(fro, zif[H_B:2 * H_B, :]).then_inc(f_ld, 16)
            pool.wait_ge(lg_mm, 24)
            for n in range(2):
                pool.dma_start(bvo[n], A["b_in"][:, 2048 + n * W_B:2048 + (n + 1) * W_B]).then_inc(bvo_ld, 16)
            pool.dma_start(cst[:, 2, :, 0:DK], A["state_mlstm_C"][0, 0].rearrange("h k v -> k h v")).then_inc(st_ld, 16)
            pool.dma_start(cst[:, 2, :, DK:DK + 1], A["state_mlstm_n"][0, 0].rearrange("h (k j) -> k h j", j=1),
                           allow_slow_non_contiguous=True).then_inc(st_ld, 16)

            def store(dst, src):
                n_out[0] += 16
                pool.dma_start(dst, src, allow_slow_non_contiguous=True).then_inc(out_st, 16)

            pool.wait_ge(lru_y, 2 * FT)
            for s in range(2):
                store(outs[2 + 5 * s][0, 0].rearrange("(f p) -> p f", p=P), hl[:, s, :])
                for f in range(FT):
                    store(outs[3 + 5 * s][0, 0, :, f * P:(f + 1) * P].rearrange("r p -> p r"), cvn[:, s, f, :])
            pool.wait_ge(row_ready, 1)
            for s in range(2):
                store(outs[6 + 5 * s][0, 0].rearrange("(p j) -> p j", j=1), mend[0:H_B, s:s + 1])
            for s, b in ((0, 0), (1, 3)):
                pool.wait_ge(c_upd, NT - 1 + s)
                store(outs[4 + 5 * s][0, 0].rearrange("h k v -> k h v"), cst[:, b, :, 0:DK])
                store(outs[5 + 5 * s][0, 0].rearrange("h (k j) -> k h j", j=1), cst[:, b, :, DK:DK + 1])
            pool.wait_ge(y_tr, NT)
            for dst, c in ((g1b, 2), (sh2b, 3), (a2b, 4)):
                for s in range(2):
                    n = P if s == 0 else DEC
                    pool.dma_start(dst[0:n, s, :], mod_dram[s, c * D:(c + 1) * D].partition_broadcast(n)).then_inc(bc_ld, 16)
            pool.dma_start(n2b, A["norm2_w"][0].partition_broadcast(P)).then_inc(bc_ld, 16)
            for t in range(NT):
                pool.wait_ge(x1_ready, t + 1)
                pool.dma_start(x1_dram[t * P:t * P + rows(t), :], xr[0:rows(t), t % 4, :]).then_inc(x1_st[t % 4], 16)
            pool.wait_ge(o_mm, NT)
            for s in range(4):
                pool.wait_ge(x1_st[s], 16 * (3 if s == 0 else 2))
            eu, ev = A["peer_u"][0], A["peer_v"][0]

            def hold():
                pool.sem_inc(pool_turn, 1)

            def gathers(h, t, n, r):
                pool.wait_ge(idx_ready, n + 1)
                pool.wait_ge(u_free, n * TOPK + 8)
                hold()
                nc.gpsimd.tensor_copy(uidx[0:r], gidx_t[0:r, t, :]).then_inc(idx_cp, 1)
                pool.wait_ge(idx_cp, n * 2 + 1)
                hold()
                for j in range(TOPK):
                    if j >= 8:
                        pool.wait_ge(u_free, n * TOPK + (j + 1))
                        hold()
                    pool.indirect_dma_start(uring[0:r, j % 8, :], None, eu, bass.IndirectOffsetOnAxis(uidx[0:r, j:j + 1], 0))\
                        .then_inc(u_ld[j % 8], 16)
                pool.wait_ge(v_free, n * TOPK + 8)
                hold()
                nc.gpsimd.tensor_copy(vidx[0:r], gidx_t[0:r, t, :]).then_inc(idx_cp, 1)
                pool.wait_ge(idx_cp, n * 2 + 2)
                hold()
                for j in range(TOPK):
                    if j >= 8:
                        pool.wait_ge(v_free, n * TOPK + (j + 1))
                        hold()
                    pool.indirect_dma_start(vring[0:r, j % 8, :], None, ev, bass.IndirectOffsetOnAxis(vidx[0:r, j:j + 1], 0))\
                        .then_inc(v_ld[j % 8], 16)

            heads_and_tiles(pool, gathers, gathers)
            pool.wait_ge(out_st, n_out[0])

        @block.tensor
        def _(pe):
            def ada_block(b):
                pe.wait_ge(ada_ld[b % 3], 32 * (b // 3 + 1))
                if b >= 2:
                    pe.wait_ge(mod_ev, b - 1)
                out = ps[0:2, b % 2, :]
                for k in range(KD):
                    nc.tensor.matmul(out, csil[:, :, k], ada[:, b % 3, k, :], start=k == 0, stop=False)
                nc.tensor.matmul(out, ones[0:1, 0:2], abias[:, b % 3, :], start=False, stop=True).then_inc(ada_mm, 1)

            pe.wait_ge(consts, 1)
            pe.wait_ge(kt_ld, 32)
            for i in range(2):
                m = nc.tensor.transpose(ps[:, 6, i * P:(i + 1) * P], kts[:, i * P:(i + 1) * P], ident[:, :])
            m.then_inc(kt_tr, 1)
            pe.wait_ge(c_silu, 1)
            for b in range(4):
                ada_block(b)
            for t in range(NT):
                r = rows(t)
                pe.wait_ge(x_sc, t + 1)
                for j in range(2):
                    if t >= 2:
                        pe.wait_ge((x_evd, x_eva)[j], t - 1)
                    for k in range(4):
                        m = nc.tensor.transpose(ps[:, 2 + 2 * (t % 2) + j, k * P:k * P + r],
                                                xin[0:r, t, (4 * j + k) * P:(4 * j + k + 1) * P], ident[0:r, 0:r])
                    m.then_inc(x_tr, 1)
            for b in range(4, 12):
                ada_block(b)
            pe.wait_ge(mod_ev, 12)
            pe.wait_ge(x_evd, NT)
            pe.wait_ge(x_eva, NT)
            unit = [0]

            def z_bank():
                u = unit[0]
                unit[0] += 1
                if u >= 4:
                    pe.wait_ge(z_ev, u - 3)
                return u % 4

            gunit = [0]
            pe.wait_ge(kt_ready, 1)
            nblk = 0
            for b in lb:
                if b[0] == "G":
                    f = int(b[1])
                    pe.wait_ge(conv_done, f + 1)
                    if f == 0:
                        pe.wait_ge(ld_prm, n_prm[0])
                    for w in (wrd, wid):
                        for g in range(3):
                            if gunit[0] >= 4:
                                pe.wait_ge(lg_ev, gunit[0] - 3)
                            nc.tensor.matmul(ps[:, 4 + gunit[0] % 4, 0:LG], w[:, f, :], uu[f % 2][:, g * LG:(g + 1) * LG],
                                             start=True, stop=True).then_inc(lg_mm, 1)
                            gunit[0] += 1
                    continue
                pe.wait_ge(w_ld[nblk % 12], 16 * (nblk // 12 + 1))
                for g in range(3):
                    bank = z_bank()
                    for k in range(KD):
                        m = nc.tensor.matmul(ps[:, bank, 0:ZG], wblk[:, nblk % 12, k, :], hT[:, k, g * ZG:(g + 1) * ZG],
                                             start=k == 0, stop=k == KD - 1)
                    m.then_inc(z_mm, 1)
                nblk += 1
            for g in range(3):
                bank = z_bank()
                for k in range(KD):
                    m = nc.tensor.matmul(ps[0:8, bank, 0:ZG], wif[:, k, :], hT[:, k, g * ZG:(g + 1) * ZG],
                                         start=k == 0, stop=k == KD - 1)
                m.then_inc(z_mm, 1)
            pe.wait_ge(bvo_ld, 32)
            for t in range(NT):
                r = rows(t)
                for n, w in enumerate((wv, wo)):
                    bank = z_bank()
                    if t == 0:
                        pe.wait_ge(vo_ld[n], 16)
                    for k in range(KD):
                        nc.tensor.matmul(ps[0:r, bank, :], hT[:, k, t * P:t * P + r], w[:, k, :], start=k == 0, stop=False)
                    nc.tensor.matmul(ps[0:r, bank, :], ones[0:1, 0:r], bvo[n],
                                     start=False, stop=True).then_inc(z_mm, 1)
            pe.wait_ge(row_exp, 1)
            pe.wait_ge(lg_ev, 24)
            for t in range(NT):
                r = rows(t)
                for a, row in enumerate((wst, nmr, wkr)):
                    nc.tensor.transpose(ps[0:r, 4, (t * 3 + a) * 4:(t * 3 + a) * 4 + 4], row[:, t * P:t * P + r],
                                        ident[0:H_B, 0:H_B])
            nc.tensor.matmul(ps[:, 4, 128:164], ones[0:H_B, :], wcd[0:H_B], start=True, stop=True).then_inc(row_tr, 1)
            pe.wait_ge(z_ev, 51 + 2 * NT)
            pe.wait_ge(col_ready, 2)

            def front(t):
                r, cs = rows(t), slice(t * P, t * P + rows(t))
                if t >= 1:
                    pe.wait_ge(p_ready, t)
                for h in range(H_B):
                    m = nc.tensor.transpose(ps[0:r, 0, h * P:(h + 1) * P], kT[:, h, cs], ident[:, :])
                m.then_inc(k_tr, 1)
                if t >= 1:
                    pe.wait_ge(d_exp, t)
                pe.wait_ge(negm_ready, t + 1)
                dst = ps[0:r, 1, :].rearrange("p (h t) -> p h t", h=H_B)[:, :, 0:r]
                nc.tensor.matmul(dst, ident[0:r, 0:r], mask[0:r, 0:r].unsqueeze(1).broadcast_to([r, H_B, r]),
                                 start=True, stop=False)
                nc.tensor.matmul(dst, aro[:, cs], seleye[:, :, 0:r], start=False, stop=False)
                nc.tensor.matmul(dst, ones[0:H_B, 0:r], negm[:, t % 2, :, 0:r], start=False, stop=True).then_inc(d_mm, 1)
                pe.wait_ge(kw_ready, t + 1)
                for h in range(H_B):
                    m = nc.tensor.matmul(ps[0:r, 0, h * P:h * P + r], kT[:, h, cs], qT[:, h, cs], start=True, stop=True)
                m.then_inc(s_mm, 1)
                if t >= 1:
                    pe.wait_ge(c_upd, t)
                for h in range(H_B):
                    m = nc.tensor.matmul(ps[:, 6 + h // 2, (h % 2) * 129:(h % 2) * 129 + 129], kw[0:r, h, :], vext[0:r, t, h, :],
                                         start=True, stop=True)
                m.then_inc(c_mm, 1)

            def back(t):
                r, cs = rows(t), slice(t * P, t * P + rows(t))
                if t >= 1:
                    pe.wait_ge(n_ev, t)
                    pe.wait_ge(nd_done, t)
                pe.wait_ge(p_ready, t + 1)
                for h in range(H_B):
                    m = nc.tensor.matmul(ps[0:r, 2 + h // 2, (h % 2) * 129:(h % 2) * 129 + 129], prob[t % 2][0:r, h, 0:r],
                                         vext[0:r, t, h, :], start=True, stop=True)
                m.then_inc(n_mm, 1)
                pe.wait_ge(c_upd, t) if t >= 1 else None
                if t == NT - 1:
                    pe.wait_ge(st_ld, 32)
                src = t % 2 if t < NT - 1 else 2
                for h in range(H_B):
                    m = nc.tensor.matmul(ps[0:r, 4 + h // 2, (h % 2) * 129:(h % 2) * 129 + 129], qT[:, h, cs], cst[:, src, h, :],
                                         start=True, stop=True)
                m.then_inc(i_mm, 1)

            front(0)
            for t in range(NT):
                if t + 1 < NT:
                    front(t + 1)
                back(t)
            pe.wait_ge(n_ev, NT)
            pe.wait_ge(p_ready, NT)
            pe.wait_ge(d_exp, NT)
            for t in range(NT):
                r = rows(t)
                pe.wait_ge(y_ready, t + 1)
                if t >= 2:
                    pe.wait_ge(y_ev, t - 1)
                for j in range(4):
                    m = nc.tensor.transpose(ps[:, t % 2, j * P:j * P + r], og[0:r, t, j * P:(j + 1) * P], ident[0:r, 0:r])
                m.then_inc(y_tr, 1)
            pe.wait_ge(wout_ld, 16)
            pe.wait_ge(y_ev, NT)
            pe.wait_ge(c_upd, NT)

            def project(t):
                r = rows(t)
                if t >= 2:
                    pe.wait_ge(x1_ready, t - 1)
                for c in range(2):
                    for k in range(KD):
                        m = nc.tensor.matmul(ps[0:r, 2 * (t % 2) + c, :], yT[:, k, t * P:t * P + r],
                                             wout[:, k, c * 512:(c + 1) * 512], start=k == 0, stop=k == KD - 1)
                m.then_inc(o_mm, 1)

            def turn_h2(t):
                r = rows(t)
                pe.wait_ge(h2_ready, t + 1)
                if t >= 2:
                    pe.wait_ge(h2_ev, t - 1)
                for k in range(KD):
                    m = nc.tensor.transpose(ps[:, 4 + 2 * (t % 2) + k // 4, (k % 4) * P:(k % 4) * P + r],
                                            h2[0:r, t, k * P:(k + 1) * P], ident[0:r, 0:r])
                m.then_inc(h2_tr, 1)

            for t in range(NT):
                project(t)
                if t >= 1:
                    turn_h2(t - 1)
            turn_h2(NT - 1)
            pe.wait_ge(h2_ev, NT)
            pe.wait_ge(x1_ready, NT)

            def hold():
                pe.sem_inc(pe_turn, 1)

            def route(t, m, r):
                pe.wait_ge(q_sb, m + 1)
                for c in range(2):
                    for k in range(KD):
                        rhs = h2T_t[:, k, t, :] if r == P else h2T[:, k, SEQ:T]
                        mm = nc.tensor.matmul(ps[:, 4, c * P:c * P + r], wqh[:, k, c * P:(c + 1) * P], rhs,
                                              start=k == 0, stop=k == KD - 1)
                mm.then_inc(q_mm, 1)
                pe.wait_ge(q_sb, m + 2)
                pe.wait_ge(r_cp, m + 1)
                hold()
                for c in range(2):
                    nc.tensor.matmul(ps[0:r, 5, c * P:(c + 1) * P], qts[:, c, 0:r], kTt[:, c, :], start=True, stop=True)
                for c in range(2):
                    mm = nc.tensor.matmul(ps[0:r, 6, 0:1], qsq[:, c, 0:r], ones[:, 0:1], start=c == 0, stop=c == 1)
                mm.then_inc(r_mm, 1)

            def mix(n, r):
                pe.wait_ge(acc_done, n + 1)
                for j in range(TOPK):
                    pe.wait_ge(dg_ready, n * TOPK + (j + 1))
                    pe.wait_ge(v_ld[j % 8], n * 32 + 16 * (j // 8 + 1))
                    hold()
                    for c in range(2):
                        mm = nc.tensor.matmul(ps[0:r, c, :], diag[0:r, j % 4, 0:r], vring[0:r, j % 8, c * 512:(c + 1) * 512],
                                              start=j == 0, stop=j == TOPK - 1)
                    mm.then_inc(v_free, 1)

            pe.sem_inc(v_free, 8)
            pe.wait_ge(wq_ld, 16)
            with pe.Fori(0, NT - 1) as t:
                route(t, t, P)
            route(NT - 1, NT - 1, DEC)

            def step(h, t, n, r):
                pe.wait_ge(wq_ld, h * 16 + 32)
                hold()
                route(t, n + NT, r)
                mix(n, r)

            heads_and_tiles(pe, step, lambda h, t, n, r: mix(n, r))

        @block.scalar
        def _(act):
            ch = Chain(act, act_step)
            for t in range(NT - 1):
                act.dma_start(xin[:, t, :], A["x_prompt"][0, t * P:(t + 1) * P, :]).then_inc(ld_x, 16)
            act.dma_start(xin[0:DEC, NT - 1, :], A["x_sample"][0]).then_inc(ld_x, 16)
            for i, nm in enumerate(("peer_k1", "peer_k2")):
                act.dma_start(kts[:, i * P:(i + 1) * P], A[nm][0]).then_inc(kt_ld, 16)
            act.wait_ge(ld_c, 32)
            nc.scalar.activation(ce, cT, ACT.Exp, scale=-1.0).then_inc(c_exp, 1)
            act.wait_ge(ld_x, 16 * NT)
            act.wait_ge(consts, 1)
            for t in range(NT):
                r = rows(t)
                if t:
                    act.wait_ge(x_sq, t)
                nc.scalar.activation(sq_junk[0:r], xin[0:r, t, :], ACT.Square, accum_out=ssq[0:r, t:t + 1]).then_inc(x_sq, 1)
            act.wait_ge(x_sq, NT + 1)
            nc.scalar.activation(ssq, ssq, ACT.Sqrt).then_inc(x_rt, 1)
            act.wait_ge(kt_tr, 1)
            nc.scalar.activation(kTt[:, :, :], ps[:, 6, 0:256].rearrange("p (c k) -> p c k", c=2), ACT.Copy).then_inc(kt_ready, 1)
            act.wait_ge(mul1_ready, 1)
            for t in range(NT):
                r = rows(t)
                act.wait_ge(x_tr, 2 * t + 2)
                s = stream(t)
                for k in range(4):
                    m = nc.scalar.activation(hT[:, 4 + k, t * P:t * P + r], ps[:, 3 + 2 * (t % 2), k * P:k * P + r], ACT.Identity,
                                             scale=mul1[:, s, 4 + k:5 + k], bias=modT[:, 0, s, 4 + k:5 + k])
                m.then_inc(x_eva, 1)
            act.wait_ge(lam_abs, 1)
            nc.scalar.activation(lt1, lt1, ACT.Exp, scale=-1.0).then_inc(lam_exp, 1)
            act.wait_ge(c8_ready, 1)
            unit = 0

            def evac_z(b):
                nonlocal unit
                kind, j, cb = blk(b)
                if kind == "xa":
                    dst, off = xpad[j % 2], PAD
                    if j >= 2:
                        act.wait_ge(conv_done, j - 1)
                elif kind == "ga":
                    dst, off = ga[j % 2], 0
                    if j >= 2:
                        act.wait_ge(lru_y, 2 * (j - 1))
                else:
                    dst, off = (qT if kind == "q" else kT)[:, j, :], 0
                gap = PAD if kind in ("xa", "ga") else 0
                scale, bias = (DK ** -0.5, binq[:, j:j + 1]) if kind == "q" else (1.0, binT[:, cb:cb + 1])
                for g in range(3):
                    act.wait_ge(z_mm, unit + 1)
                    c0 = g * ZG
                    n = min(ZG, SEQ - c0)
                    m = nc.scalar.activation(dst[:, off + c0:off + c0 + n], ps[:, unit % 4, 0:n], ACT.Identity, scale=scale, bias=bias)
                    if n < ZG:
                        m = nc.scalar.activation(dst[:, off + SEQ + gap:off + gap + T], ps[:, unit % 4, n:ZG], ACT.Identity,
                                                 scale=scale, bias=bias)
                    m.then_inc(z_ev, 1)
                    unit += 1

            def gates(f):
                if f:
                    act.wait_ge(lru_scan, f)
                for w, (dst, bias) in enumerate(((rr, nbr), (ii, nbi))):
                    for g in range(3):
                        v = f * 6 + w * 3 + g
                        act.wait_ge(lg_mm, v + 1)
                        nc.scalar.activation(dst[:, g * LG:(g + 1) * LG], ps[:, 4 + v % 4, 0:LG], ACT.Exp, scale=-1.0,
                                             bias=bias[:, f:f + 1]).then_inc(lg_ev, 1)

            def decays(f):
                act.wait_ge(rg_ready, f + 1)
                if f:
                    act.wait_ge(lru_scan, f)
                ch.link(nc.scalar.activation(aa[:, 0:UL], rr[:, 0:UL], ACT.Exp, scale=nc8[:, f:f + 1]))
                nc.scalar.activation(rr[:, 0:UL], rr[:, 0:UL], ACT.Tanh, scale=c8[:, f:f + 1]).then_inc(lru_ac, 1)

            def roots(f):
                act.wait_ge(lru_d3, f + 1)
                nc.scalar.activation(pp[:, 0:UL], pp[:, 0:UL], ACT.Exp, scale=-GELU_S).then_inc(lru_d4a, 1)
                nc.scalar.activation(dd[:, 0:UL], dd[:, 0:UL], ACT.Sqrt).then_inc(lru_d4a, 1)

            after = {"xa1": [], "G0": [(gates, 0)], "ga1": [(decays, 0)], "xa2": [(roots, 0)], "G1": [(gates, 1)],
                     "ga2": [(decays, 1)], "xa3": [(roots, 1)], "G2": [(gates, 2)], "ga3": [(decays, 2)], "q0": [(roots, 2)],
                     "G3": [(gates, 3)], "q1": [(decays, 3)], "q2": [(roots, 3)]}
            for b in lb:
                if b[0] != "G":
                    evac_z(b)
                for fn, f in after.get(b, []):
                    fn(f)
            act.wait_ge(lru_y, 2 * FT)
            for g in range(3):
                act.wait_ge(z_mm, unit + 1)
                nc.scalar.activation(zif[:, g * ZG:(g + 1) * ZG], ps[0:8, unit % 4, 0:ZG], ACT.Identity,
                                     bias=bif[0:8]).then_inc(z_ev, 1)
                unit += 1

            def evac_vo(t):
                nonlocal unit
                r = rows(t)
                act.wait_ge(z_mm, unit + 1)
                nc.scalar.activation(vext[0:r, t, :, 0:DK], ps[0:r, unit % 4, :].rearrange("p (h e) -> p h e", h=H_B),
                                     ACT.Copy).then_inc(z_ev, 1)
                act.wait_ge(z_mm, unit + 2)
                nc.scalar.activation(og[0:r, t, :], ps[0:r, (unit + 1) % 4, :], ACT.Exp, scale=-1.0).then_inc(z_ev, 1)
                unit += 2

            for t in range(NT):
                evac_vo(t)
                if t == 2:
                    act.wait_ge(f_abs, 1)
                    nc.scalar.activation(nmr, wst, ACT.Exp, scale=-1.0).then_inc(f_exp, 1)
            act.wait_ge(row_ready, 1)
            for w in (wst, nmr, wkr):
                ch.link(nc.scalar.activation(w, w, ACT.Exp))
            nc.scalar.activation(wcr[0:H_B], wcr[0:H_B], ACT.Exp).then_inc(f_exp, 1)
            for t in range(NT):
                r = rows(t)

                def decay_exp(t):
                    r = rows(t)
                    act.wait_ge(d_mm, t + 1)
                    if t >= 2:
                        act.wait_ge(p_ready, t - 1)
                    nc.scalar.activation(decay[t % 2][0:r, :, 0:r], ps[0:r, 1, :].rearrange("p (h t) -> p h t", h=H_B)[:, :, 0:r],
                                         ACT.Exp).then_inc(d_exp, 1)
                if t == 0:
                    decay_exp(0)
                if t + 1 < NT:
                    decay_exp(t + 1)
                act.wait_ge(n_mm, t + 1)
                if t >= 2:
                    act.wait_ge(h_ready, t - 1)
                for b in range(2):
                    m = nc.scalar.activation(nd[t % 2][0:r, 2 * b:2 * b + 2, :],
                                             ps[0:r, 2 + b, 0:258].rearrange("p (h e) -> p h e", h=2), ACT.Copy)
                m.then_inc(n_ev, 1)
                act.wait_ge(h_ready, t + 1)
                for h in range(H_B):
                    if t or h:
                        act.wait_ge(h_sq, 4 * t + h)
                    m = nc.scalar.activation(kwj[0:r], hh[0:r, t, h * P:(h + 1) * P], ACT.Square,
                                             accum_out=ssqh[0:r, 4 * t + h:4 * t + h + 1]).then_inc(h_sq, 1)
            act.wait_ge(h_rt, 1)
            nc.scalar.activation(ssqh, ssqh, ACT.Sqrt).then_inc(h_rt, 1)
            for t in range(NT):
                r = rows(t)
                act.wait_ge(y_tr, t + 1)
                nc.scalar.activation(yT[:, 4:8, t * P:t * P + r],
                                     ps[:, t % 2, :].rearrange("p (j t) -> p j t", j=4)[:, :, 0:r], ACT.Copy).then_inc(y_ev, 1)

            def turn(t):
                r = rows(t)
                act.wait_ge(h2_tr, t + 1)
                for j in range(2):
                    m = nc.scalar.activation(h2T[:, 4 * j:4 * j + 4, t * P:t * P + r],
                                             ps[:, 4 + 2 * (t % 2) + j, :].rearrange("p (k t) -> p k t", k=4)[:, :, 0:r], ACT.Copy)
                m.then_inc(h2_ev, 1)

            for t in range(NT):
                r = rows(t)
                act.wait_ge(x1_ready, t + 1)
                if t >= 1:
                    act.wait_ge(x1_sq, t)
                nc.scalar.activation(sq2[0:r], xr[0:r, t % 4, :], ACT.Square, accum_out=ssq2[0:r, t:t + 1]).then_inc(x1_sq, 1)
                act.wait_ge(x1_rt, 2 * t + 1)
                nc.scalar.activation(rstd2[0:r, t:t + 1], rstd2[0:r, t:t + 1], ACT.Sqrt).then_inc(x1_rt, 1)
                if t >= 1:
                    turn(t - 1)
            turn(NT - 1)
            for s in range(4):
                act.wait_ge(x1_st[s], 16 * (3 if s == 0 else 2))
            act.wait_ge(h2_ready, NT)

            def hold():
                act.sem_inc(act_turn, 1)

            def query(m, r):
                act.wait_ge(q_mm, m + 1)
                act.wait_ge(r_mm, m + 1)
                for dst, fn in ((qts, ACT.Copy), (qsq, ACT.Square)):
                    last = nc.scalar.activation(dst[:, :, 0:r], ps[:, 4, 0:256].rearrange("p (c t) -> p c t", c=2)[:, :, 0:r], fn)
                last.then_inc(q_sb, 1)
                act.wait_ge(r_mm, m + 2)
                act.wait_ge(r_cp, m + 1)
                nc.scalar.activation(qrt[0:r], ps[0:r, 6, 0:1], ACT.Sqrt, scale=1.0 / DQ, bias=epsc[0:r]).then_inc(q_rt, 1)

            def softmax(m, r):
                act.wait_ge(p_in, m + 2)
                nc.scalar.activation(pexp[0:r], sv[0:r], ACT.Exp, scale=qrs[0:r], bias=nsv0[0:r],
                                     accum_out=psm[0:r]).then_inc(p_exp, 1)

            def weights(n, r, m=None):
                act.wait_ge(g_in, n + 1)
                nc.scalar.activation(gl2[0:r], gl[0:r], ACT.Exp, scale=-GELU_S).then_inc(g_exp, 1)
                act.wait_ge(w_ready, n + 1)
                for j in range(TOPK):
                    act.wait_ge(v_free, n * TOPK + (j + 5))
                    nc.scalar.activation(diag[0:r, j % 4, 0:r], ident[0:r, 0:r], ACT.Copy, scale=wgt[0:r, j:j + 1])\
                        .then_inc(dg_ready, 1)
                    if j == 7 and m is not None:
                        softmax(m, r)

            act.sem_inc(q_sb, 1)
            act.sem_inc(r_mm, 1)
            with act.Fori(0, NT - 1) as t:
                query(t, P)
                softmax(t, P)
            query(NT - 1, DEC)
            softmax(NT - 1, DEC)

            def step(h, t, n, r):
                query(n + NT, r)
                weights(n, r, n + NT)

            def last_step(h, t, n, r):
                weights(n, r)
                act.wait_ge(f_var, t * 2 + 1)
                hold()
                nc.scalar.activation(fdump[0:r], acc[0:r, t, :], ACT.Square, accum_out=fss[0:r]).then_inc(f_sq, 1)
                act.wait_ge(f_var, t * 2 + 2)
                nc.scalar.activation(frs[0:r], frs[0:r], ACT.Sqrt).then_inc(f_rt, 1)

            heads_and_tiles(act, step, last_step)

        @block.vector
        def _(dve):
            V = nc.vector
            ch = Chain(dve, dve_step)
            link = ch.link
            dve.wait_ge(c_exp, 1)
            link(V.tensor_scalar(ce, ce, 1.0, None, ALU.add))
            link(V.reciprocal(ce, ce))
            V.tensor_tensor(csil, cT, ce, ALU.mult).then_inc(c_silu, 1)
            for b in range(4):
                dve.wait_ge(ada_mm, b + 1)
                if b >= 2:
                    dve.wait_ge(mod_st[b % 2], 16 * (b // 2))
                V.tensor_copy(modrow[:, b % 2, :], ps[0:2, b % 2, :]).then_inc(mod_ev, 1)
            dve.wait_ge(x_sq, NT)
            V.tensor_scalar(ssq, ssq, 1.0 / D, EPS, ALU.mult, ALU.add).then_inc(x_sq, 1)
            dve.wait_ge(x_rt, 1)
            link(V.reciprocal(rstd1, ssq))
            for t in range(NT):
                r = rows(t)
                V.tensor_scalar(xin[0:r, t, :], xin[0:r, t, :], rstd1[0:r, t:t + 1], None, ALU.mult).then_inc(x_sc, 1)
            dve.wait_ge(ld_prm, n_prm[0])
            dve.wait_ge(ld_modT, 64)
            for s in range(2):
                m = V.scalar_tensor_tensor(mul1[:, s, :], modT[:, 1, s, :], 1.0, n1T, ALU.add, ALU.mult)
                if s:
                    m.then_inc(mul1_ready, 1)
                else:
                    link(m)
            dve.wait_ge(mul1_ready, 1)
            for t in range(NT):
                r, s = rows(t), stream(t)
                dve.wait_ge(x_tr, 2 * t + 1)
                for k in range(4):
                    m = V.tensor_scalar(hT[:, k, t * P:t * P + r], ps[:, 2 + 2 * (t % 2), k * P:k * P + r], mul1[:, s, k:k + 1],
                                        modT[:, 0, s, k:k + 1], ALU.mult, ALU.add)
                m.then_inc(x_evd, 1)
            V.scalar_tensor_tensor(lt1, lam, -1.0, lam, ALU.mult, ALU.max).then_inc(lam_abs, 1)

            def log1p(y, w, p):
                link(V.tensor_scalar(w, y, 2.0, None, ALU.add))
                link(V.reciprocal(w, w))
                link(V.tensor_tensor(y, y, w, ALU.mult))
                link(V.tensor_tensor(w, y, y, ALU.mult))
                link(V.tensor_scalar(p, w, LOG1P[-1], None, ALU.mult))
                for c in reversed(LOG1P[:-1]):
                    link(V.scalar_tensor_tensor(p, p, c, w, ALU.add, ALU.mult))
                link(V.scalar_tensor_tensor(p, p, 1.0, y, ALU.add, ALU.mult))
                link(V.tensor_scalar(p, p, 2.0, None, ALU.mult))

            dve.wait_ge(lam_exp, 1)
            log1p(lt1, lt2, c8)
            link(V.tensor_scalar(lt1, lam, -1.0, 0.0, ALU.mult, ALU.max))
            link(V.tensor_tensor(c8, c8, lt1, ALU.add))
            link(V.tensor_scalar(c8, c8, LRU_C, None, ALU.mult))
            link(V.tensor_scalar(nc8, c8, -1.0, None, ALU.mult))
            link(V.tensor_scalar(nbr, nbr, -1.0, None, ALU.mult))
            link(V.tensor_scalar(nbi, nbi, -1.0, None, ALU.mult))
            for b in range(4, 12):
                dve.wait_ge(ada_mm, b + 1)
                dve.wait_ge(mod_st[b % 2], 16 * (b // 2))
                V.tensor_copy(modrow[:, b % 2, :], ps[0:2, b % 2, :]).then_inc(mod_ev, 1)
            dve.wait_ge(x_tr, 2 * NT)
            for i in range(2):
                link(V.memset(xpad[i][:, 0:PAD], 0.0))
                link(V.memset(ga[i][:, SEQ:SEQ + PAD], 0.0))
            V.tensor_scalar(binq, binT[:, 8:12], DK ** -0.5, None, ALU.mult).then_inc(c8_ready, 1)

            def conv(f):
                x, u = xpad[f % 2], uu[f % 2][:, 0:UL]
                link(V.tensor_copy(x[:, PAD + SEQ:2 * PAD + SEQ], cv0[:, f, :]))
                dve.wait_ge(z_ev, 3 * (zblocks.index(f"xa{f}") + 1))
                link(V.tensor_scalar(u, x[:, 0:UL], convw[:, 0, f:f + 1], convb[:, f:f + 1], ALU.mult, ALU.add))
                for k in range(1, CONV_W):
                    link(V.scalar_tensor_tensor(u, x[:, k:k + UL], convw[:, k, f:f + 1], u, ALU.mult, ALU.add))
                link(V.tensor_copy(cvn[:, 0, f, :], x[:, SEQ:SEQ + PAD]))
                V.tensor_copy(cvn[:, 1, f, :], x[:, UL:XL]).then_inc(conv_done, 1)

            def gate_values(f):
                r, i, u = rr[:, 0:UL], ii[:, 0:UL], uu[f % 2][:, 0:UL]
                dve.wait_ge(lg_ev, 6 * f + 3)
                link(V.tensor_scalar(r, r, 1.0, None, ALU.add))
                V.reciprocal(r, r).then_inc(rg_ready, 1)
                dve.wait_ge(lg_ev, 6 * f + 6)
                link(V.tensor_scalar(i, i, 1.0, None, ALU.add))
                link(V.reciprocal(i, i))
                link(V.tensor_tensor(i, i, u, ALU.mult))

            def inner(f):
                th, d, p, g = rr[:, 0:UL], dd[:, 0:UL], pp[:, 0:UL], ga[f % 2][:, 0:UL]
                dve.wait_ge(z_ev, 3 * (zblocks.index(f"ga{f}") + 1))
                link(V.tensor_tensor(p, g, g, ALU.mult))
                link(V.tensor_scalar(p, p, GELU_C, 1.0, ALU.mult, ALU.add))
                link(V.tensor_tensor(p, p, g, ALU.mult))
                link(V.tensor_scalar(p, p, EXP_MAX / -GELU_S, None, ALU.max))
                dve.wait_ge(lru_ac, f + 1)
                link(V.tensor_scalar(d, th, 1.0, None, ALU.add))
                link(V.reciprocal(d, d))
                V.scalar_tensor_tensor(d, th, 2.0, d, ALU.mult, ALU.mult).then_inc(lru_d3, 1)

            def outer(f):
                i, a, d, p, u, g = ii[:, 0:UL], aa[:, 0:UL], dd[:, 0:UL], pp[:, 0:UL], uu[f % 2][:, 0:UL], ga[f % 2][:, 0:UL]
                s0 = SEQ + PAD
                dve.wait_ge(lru_d4a, 2 * f + 1)
                link(V.tensor_scalar(p, p, 1.0, None, ALU.add))
                link(V.reciprocal(p, p))
                link(V.tensor_tensor(p, p, g, ALU.mult))
                dve.wait_ge(lru_d4a, 2 * f + 2)
                V.tensor_tensor(i, i, d, ALU.mult).then_inc(lru_bx, 1)
                dve.wait_ge(lru_bx, f + 1)
                link(V.tensor_tensor_scan(u[:, 0:SEQ], a[:, 0:SEQ], i[:, 0:SEQ], 0.0, ALU.mult, ALU.add))
                V.tensor_tensor_scan(u[:, s0:UL], a[:, s0:UL], i[:, s0:UL], h0T[:, f:f + 1], ALU.mult, ALU.add).then_inc(lru_scan, 1)
                dve.wait_ge(lru_scan, f + 1)
                link(V.tensor_copy(hl[:, 0, f:f + 1], u[:, SEQ - 1:SEQ]))
                link(V.tensor_copy(hl[:, 1, f:f + 1], u[:, UL - 1:UL]))
                V.tensor_tensor(yT[:, f, 0:SEQ], u[:, 0:SEQ], p[:, 0:SEQ], ALU.mult).then_inc(lru_y, 1)
                V.tensor_tensor(yT[:, f, SEQ:T], u[:, s0:UL], p[:, s0:UL], ALU.mult).then_inc(lru_y, 1)
                dve.wait_ge(lru_y, 2 * f + 2)

            dve.wait_ge(c8_ready, 1)
            for i in range(2):
                dve.wait_ge(mod_st[i], 96)
            conv(0)
            for f in range(FT):
                gate_values(f)
                if f + 1 < FT:
                    conv(f + 1)
                inner(f)
                outer(f)
            dve.wait_ge(f_ld, 16)
            dve.wait_ge(z_mm, 48)
            V.scalar_tensor_tensor(wst, fro, -1.0, fro, ALU.mult, ALU.max).then_inc(f_abs, 1)
            dve.wait_ge(f_exp, 1)
            log1p(nmr, wkr, wst)
            link(V.scalar_tensor_tensor(fro, fro, 0.0, wst, ALU.min, ALU.subtract))
            for t in range(NT):
                c = slice(t * P, t * P + rows(t))
                link(V.tensor_tensor_scan(wst[:, c], ones[0:H_B, 0:rows(t)], fro[:, c], 0.0, ALU.mult, ALU.add))
            link(V.tensor_tensor(aro, zif[0:H_B, :], wst, ALU.subtract))
            link(V.memset(mprev[0:H_B, 0:1], 0.0))
            for t in range(NT):
                c, e = slice(t * P, t * P + rows(t)), t * P + rows(t)
                link(V.tensor_tensor_scan(mro[:, c], aro[:, c], aro[:, c], mprev[0:H_B, t:t + 1], ALU.max, ALU.max))
                nxt = mprev[0:H_B, t + 1:t + 2] if t < NT - 2 else mend[0:H_B, stream(t):stream(t) + 1]
                link(V.tensor_tensor(nxt, wst[:, e - 1:e], mro[:, e - 1:e], ALU.add))
                link(V.tensor_copy(mlast[0:H_B, t:t + 1], mro[:, e - 1:e]))
            link(V.scalar_tensor_tensor(nmr, wst, -1.0, mro, ALU.mult, ALU.subtract))
            for t in range(NT):
                c = slice(t * P, t * P + rows(t))
                link(V.tensor_scalar(wst[:, c], mro[:, c], mprev[0:H_B, t:t + 1], -1.0, ALU.subtract, ALU.mult))
                link(V.tensor_scalar(wkr[:, c], aro[:, c], mlast[0:H_B, t:t + 1], None, ALU.subtract))
            V.tensor_tensor(wcr[0:H_B], mprev[0:H_B], mlast[0:H_B], ALU.subtract).then_inc(row_ready, 1)
            dve.wait_ge(f_exp, 2)
            V.tensor_tensor(wcd[0:H_B], seleye[:, :, 0].unsqueeze(1).broadcast_to([H_B, NT, H_B]),
                            wcr[0:H_B].unsqueeze(2).broadcast_to([H_B, NT, H_B]), ALU.mult).then_inc(row_exp, 1)
            dve.wait_ge(z_ev, 51 + 2 * NT)
            for t in range(NT):
                r = rows(t)
                link(V.memset(vext[0:r, t, :, DK:DK + 1], 1.0))
                link(V.tensor_scalar(og[0:r, t, :], og[0:r, t, :], 1.0, None, ALU.add))
                link(V.reciprocal(og[0:r, t, :], og[0:r, t, :]))
                link(V.tensor_tensor(og[0:r, t, :], og[0:r, t, :], nwb[0:r, :], ALU.mult))
            dve.wait_ge(row_tr, 1)
            link(V.memset(cst[:, 0, :, :], 0.0))
            link(V.tensor_copy(wcb, ps[:, 4, 128:164].rearrange("p (c h) -> p c h", c=NT)))
            V.tensor_copy(colT[:, 0:NT - 1], ps[:, 4, 0:12 * (NT - 1)].rearrange("p (t a h) -> p t a h", a=3, h=H_B)).then_inc(col_ready, 1)
            V.tensor_copy(colT[0:DEC, NT - 1], ps[0:DEC, 4, 12 * (NT - 1):12 * NT].rearrange("p (a h) -> p a h", a=3)).then_inc(col_ready, 1)
            dve.wait_ge(col_ready, 2)

            def front(t):
                r, c = rows(t), slice(t * P, t * P + rows(t))
                if t >= 2:
                    dve.wait_ge(d_mm, t - 1)
                V.scalar_tensor_tensor(negm[:, t % 2, :, 0:r], mro[:, c].unsqueeze(1).broadcast_to([H_B, H_B, r]), -1.0,
                                       seleye[:, :, 0:r], ALU.mult, ALU.mult).then_inc(negm_ready, 1)
                dve.wait_ge(k_tr, t + 1)
                if t >= 1:
                    dve.wait_ge(c_mm, t)
                V.tensor_tensor(kw[0:r], ps[0:r, 0, :].rearrange("p (h d) -> p h d", h=H_B),
                                colT[0:r, t, 2, :].unsqueeze(2).broadcast_to([r, H_B, P]), ALU.mult).then_inc(kw_ready, 1)
                dve.wait_ge(s_mm, t + 1)
                dve.wait_ge(d_exp, t + 1)
                if t >= 2:
                    dve.wait_ge(n_mm, t - 1)
                V.tensor_tensor(prob[t % 2][0:r, :, 0:r], ps[0:r, 0, :].rearrange("p (h t) -> p h t", h=H_B)[:, :, 0:r],
                                decay[t % 2][0:r, :, 0:r], ALU.mult).then_inc(p_ready, 1)

            def carry(t):
                src, dst = (t % 2, (t + 1) % 2) if t < NT - 1 else (2, 3)
                dve.wait_ge(c_mm, t + 1)
                if 1 <= t < NT - 1:
                    dve.wait_ge(i_mm, t)
                if t == NT - 1:
                    dve.wait_ge(st_ld, 32)
                for h in range(H_B):
                    m = V.scalar_tensor_tensor(cst[:, dst, h, :], cst[:, src, h, :], wcb[:, t, h:h + 1],
                                               ps[:, 6 + h // 2, (h % 2) * 129:(h % 2) * 129 + 129], ALU.mult, ALU.add)
                    if h < H_B - 1:
                        link(m)
                    else:
                        m.then_inc(c_upd, 1)
                        dve.wait_ge(c_upd, t + 1)

            def back(t):
                r = rows(t)
                n = nd[t % 2]
                dve.wait_ge(n_ev, t + 1)
                dve.wait_ge(i_mm, t + 1)
                for h in range(H_B):
                    m = V.scalar_tensor_tensor(n[0:r, h, :], ps[0:r, 4 + h // 2, (h % 2) * 129:(h % 2) * 129 + 129],
                                               colT[0:r, t, 0, h:h + 1], n[0:r, h, :], ALU.mult, ALU.add)
                    if h < H_B - 1:
                        link(m)
                    else:
                        m.then_inc(nd_done, 1)
                        dve.wait_ge(nd_done, t + 1)
                link(V.scalar_tensor_tensor(den[0:r], n[0:r, :, DK], -1.0, n[0:r, :, DK], ALU.mult, ALU.max))
                link(V.tensor_tensor(den[0:r], den[0:r], colT[0:r, t, 1, :], ALU.max))
                link(V.reciprocal(rden[0:r], den[0:r]))
                V.tensor_tensor(hh[0:r, t, :].rearrange("p (h e) -> p h e", h=H_B), n[0:r, :, 0:DK],
                                rden[0:r].unsqueeze(2).broadcast_to([r, H_B, DK]), ALU.mult).then_inc(h_ready, 1)
                dve.wait_ge(h_ready, t + 1)

            front(0)
            for t in range(NT):
                if t + 1 < NT:
                    front(t + 1)
                carry(t)
                back(t)
            dve.wait_ge(h_sq, 4 * NT)
            V.tensor_scalar(ssqh, ssqh, 1.0 / DK, EPS, ALU.mult, ALU.add).then_inc(h_rt, 1)
            dve.wait_ge(h_rt, 2)
            link(V.reciprocal(rsth, ssqh))
            for t in range(NT):
                r = rows(t)
                for h in range(H_B):
                    m = V.scalar_tensor_tensor(og[0:r, t, h * P:(h + 1) * P], hh[0:r, t, h * P:(h + 1) * P],
                                               rsth[0:r, 4 * t + h:4 * t + h + 1], og[0:r, t, h * P:(h + 1) * P], ALU.mult, ALU.mult)
                    if h < H_B - 1:
                        link(m)
                m.then_inc(y_ready, 1)
            dve.wait_ge(bc_ld, 16 * 7)
            for s in range(2):
                n = P if s == 0 else DEC
                m = V.scalar_tensor_tensor(a2b[0:n, s, :], a2b[0:n, s, :], 1.0, n2b[0:n, :], ALU.add, ALU.mult)
                link(m)

            for t in range(NT):
                r, s = rows(t), stream(t)
                x = xr[0:r, t % 4, :]
                dve.wait_ge(o_mm, t + 1)
                dve.wait_ge(xr_ld[t % 4], 16 * (t // 4 + 1))
                o = ps[0:r, 2 * (t % 2):2 * (t % 2) + 2, :].rearrange("p b n -> p (b n)")
                link(V.tensor_tensor(h2[0:r, t, :], o, g1b[0:r, s, :], ALU.mult))
                V.tensor_tensor(x, x, h2[0:r, t, :], ALU.add).then_inc(x1_ready, 1)
                dve.wait_ge(x1_sq, t + 1)
                V.tensor_scalar(rstd2[0:r, t:t + 1], ssq2[0:r, t:t + 1], 1.0 / D, EPS, ALU.mult, ALU.add).then_inc(x1_rt, 1)
                dve.wait_ge(x1_rt, 2 * t + 2)
                link(V.reciprocal(rstd2[0:r, t:t + 1], rstd2[0:r, t:t + 1]))
                link(V.scalar_tensor_tensor(h2[0:r, t, :], x, rstd2[0:r, t:t + 1], a2b[0:r, s, :], ALU.mult, ALU.mult))
                V.tensor_tensor(h2[0:r, t, :], h2[0:r, t, :], sh2b[0:r, s, :], ALU.add).then_inc(h2_ready, 1)
            dve.wait_ge(h2_ready, NT)
            dve.wait_ge(x1_sq, NT)
            for s in range(4):
                dve.wait_ge(x1_st[s], 16 * (3 if s == 0 else 2))
            link(V.memset(acc, 0.0))
            link(V.memset(epsc, EPS))
            dve.sem_inc(u_free, 8)
            dve.sem_inc(r_cp, 1)
            dve.sem_inc(acc_done, 1)
            dve.sem_inc(p_in, 1)
            rc, mc, fc = Chain(dve, route_step), Chain(dve, mix_step), Chain(dve, fin_step)

            def hold():
                dve.sem_inc(dve_turn, 1)

            def top8(out, idx, src, rest):
                V.max_index(idx, out, src)
                return V.match_replace(rest, out, src, NEG_MAX)

            def route(t, m, r, again=True):
                rc.base, rc.n = m * K_ROUTE, 0
                s2 = [slice(c * P, (c + 1) * P) for c in range(2)]
                lo = [slice(c * TOPK, c * TOPK + 8) for c in range(2)]
                hi = [slice(c * TOPK + 8, c * TOPK + 16) for c in range(2)]
                sc = ps[0:r, 5, 0:256]
                dve.wait_ge(r_mm, m + 2)
                hold()
                V.max(top[0:r, lo[0]], sc[:, s2[0]])
                rc.link(V.max(top[0:r, lo[1]], sc[:, s2[1]]))
                hold()
                for c in range(2):
                    last = top8(top[0:r, lo[c]], topi[0:r, lo[c]], sc[:, s2[c]], swk[0:r, s2[c]])
                rc.link(last)
                hold()
                V.max(top[0:r, hi[0]], swk[0:r, s2[0]])
                rc.link(V.max(top[0:r, hi[1]], swk[0:r, s2[1]]))
                hold()
                for c in range(2):
                    V.max_index(topi[0:r, hi[c]], top[0:r, hi[c]], swk[0:r, s2[c]])
                rc.link(V.tensor_tensor(cand[0:r].rearrange("p (a b) -> p a b", a=TOPK),
                                        top[0:r, 0:TOPK].unsqueeze(2).broadcast_to([r, TOPK, TOPK]),
                                        top[0:r, TOPK:2 * TOPK].unsqueeze(1).broadcast_to([r, TOPK, TOPK]), ALU.add))
                hold()
                V.max(sv[0:r, 0:8], cand[0:r])
                dve.wait_ge(q_rt, m + 1)
                V.reciprocal(qrs[0:r], qrt[0:r]).then_inc(r_cp, 1)
                rc.link(V.tensor_copy(topf[0:r], topi[0:r]))
                hold()
                rc.link(top8(sv[0:r, 0:8], si[0:r, 0:8], cand[0:r], cand2[0:r]))
                hold()
                V.tensor_scalar(nsv0[0:r], sv[0:r, 0:1], -1.0, qrs[0:r], ALU.mult, ALU.mult)
                rc.link(V.max(sv[0:r, 8:16], cand2[0:r]))
                hold()
                V.max_index(si[0:r, 8:16], sv[0:r, 8:16], cand2[0:r]).then_inc(p_in, 1)
                dve.wait_ge(p_in, m + 2)
                V.tensor_scalar(sab[0:r, 0:TOPK], si[0:r], 4, None, ALU.logical_shift_right)
                rc.link(V.tensor_scalar(sab[0:r, TOPK:2 * TOPK], si[0:r], 15, None, ALU.bitwise_and))
                rc.link(V.tensor_copy(sabf[0:r], sab[0:r]))
                half = [slice(c * TOPK, (c + 1) * TOPK) for c in range(2)]
                for c in range(2):
                    last = V.tensor_tensor(hot[c][0:r], sabf[0:r, half[c]].unsqueeze(2).broadcast_to([r, TOPK, TOPK]),
                                           pos16[0:r].unsqueeze(1).broadcast_to([r, TOPK, TOPK]), ALU.is_equal)
                rc.link(last)
                for c in range(2):
                    last = V.tensor_tensor(hot[c][0:r], hot[c][0:r],
                                           topf[0:r, half[c]].unsqueeze(1).broadcast_to([r, TOPK, TOPK]), ALU.mult)
                rc.link(last)
                for c in range(2):
                    last = V.tensor_reduce(e12[0:r, half[c]], hot[c][0:r], AXX, ALU.add)
                rc.link(last)
                if again:
                    dve.wait_ge(idx_cp, m * 2 + (2 - 2 * NT))
                V.scalar_tensor_tensor(gidx_t[0:r, t, :], e12[0:r, half[0]], float(P), e12[0:r, half[1]],
                                       ALU.mult, ALU.add).then_inc(idx_ready, 1)
                dve.wait_ge(p_exp, m + 1)
                rc.link(V.reciprocal(prs[0:r], psm[0:r]))
                rc.link(V.tensor_scalar(gate_t[0:r, t, :], pexp[0:r], prs[0:r], None, ALU.mult))
                assert rc.n == K_ROUTE, rc.n

            def dot_products(t, n, r):
                for j in range(TOPK):
                    dve.wait_ge(u_ld[j % 8], n * 32 + 16 * (j // 8 + 1))
                    dve.wait_ge(u_free, n * TOPK + (j + 7))
                    V.scalar_tensor_tensor(udump[j % 2][0:r], uring[0:r, j % 8, :], 1.0, h2[0:r, t, :], ALU.mult, ALU.mult,
                                           accum_out=dots[0:r, j:j + 1]).then_inc(u_free, 1)
                dve.wait_ge(u_free, n * TOPK + (TOPK + 8))

            def expert_weights(t, n, r):
                mc.base, mc.n = n * K_MIX, 0
                d, g = dots[0:r], gl[0:r]
                mc.link(V.tensor_tensor(g, d, d, ALU.mult))
                mc.link(V.tensor_scalar(g, g, GELU_C, 1.0, ALU.mult, ALU.add))
                mc.link(V.tensor_tensor(g, g, d, ALU.mult))
                V.tensor_scalar(g, g, EXP_MAX / -GELU_S, None, ALU.max).then_inc(g_in, 1)
                dve.wait_ge(g_exp, n + 1)
                mc.link(V.tensor_scalar(gl2[0:r], gl2[0:r], 1.0, None, ALU.add))
                mc.link(V.reciprocal(gl2[0:r], gl2[0:r]))
                mc.link(V.tensor_tensor(gl2[0:r], gl2[0:r], d, ALU.mult))
                V.tensor_tensor(wgt[0:r], gl2[0:r], gate_t[0:r, t, :], ALU.mult).then_inc(w_ready, 1)
                dve.wait_ge(w_ready, n + 1)
                assert mc.n == K_MIX, mc.n

            def accumulate(t, n, r):
                dve.wait_ge(v_free, n * TOPK + (TOPK + 8))
                V.tensor_tensor(acc[0:r, t, :], acc[0:r, t, :], ps[0:r, 0:2, :].rearrange("p b n -> p (b n)"),
                                ALU.add).then_inc(acc_done, 1)
                dve.wait_ge(acc_done, n + 2)

            def final(t, n, r):
                fc.base, fc.n = t * K_FIN, 0
                a = acc[0:r, t, :]
                s = 0 if r == P else 1
                dve.wait_ge(g2_ld, 48)
                fc.link(V.tensor_tensor(a, a, g2b[0:r, s, :], ALU.mult))
                dve.wait_ge(x1_ld, t * 16 + 16)
                V.tensor_tensor(a, a, x1s[0:r], ALU.add).then_inc(f_var, 1)
                dve.wait_ge(f_sq, t + 1)
                V.tensor_scalar(frs[0:r], fss[0:r], 1.0 / D, EPS, ALU.mult, ALU.add).then_inc(f_var, 1)
                dve.wait_ge(f_rt, t + 1)
                fc.link(V.reciprocal(frs[0:r], frs[0:r]))
                dve.wait_ge(y_st, t * 16 + 16)
                V.scalar_tensor_tensor(ys[0:r], a, frs[0:r], fwb[0:r, :], ALU.mult, ALU.mult).then_inc(y_out, 1)
                assert fc.n == K_FIN, fc.n

            with dve.Fori(0, NT - 1) as t:
                route(t, t, P, again=False)
            route(NT - 1, NT - 1, DEC, again=False)

            def step(h, t, n, r):
                dot_products(t, n, r)
                expert_weights(t, n, r)
                route(t, n + NT, r)
                accumulate(t, n, r)

            def last_step(h, t, n, r):
                dot_products(t, n, r)
                expert_weights(t, n, r)
                accumulate(t, n, r)
                final(t, n, r)

            heads_and_tiles(dve, step, last_step)


def kernel(**inputs):
    import numpy as _np
    import concourse.bacc as _bacc
    from concourse.bass_utils import run_bass_kernel_spmd as _run

    nc = _bacc.Bacc("TRN2", target_bir_lowering=False, num_devices=1)
    arrays, A = {}, {}
    for name, a in inputs.items():
        a = _np.ascontiguousarray(a)
        arrays[f"in_{name}"] = a
        A[name] = nc.dram_tensor(f"in_{name}", a.shape, mybir.dt.from_np(a.dtype), kind="ExternalInput").ap()
    outs = [nc.dram_tensor(f"out_{i}", s, F32, kind="ExternalOutput").ap() for i, s in enumerate(OUTS)]
    build(nc, A, outs)
    r = _run(nc, [arrays], core_ids=[0])
    return tuple(r.results[0][f"out_{i}"] for i in range(len(OUTS)))
```

```python
from contextlib import ExitStack

import concourse.bass as bass
from concourse import mybir

F32 = mybir.dt.float32
BF16 = mybir.dt.bfloat16
I32 = mybir.dt.int32
U32 = mybir.dt.uint32
ALU = mybir.AluOpType
ACT = mybir.ActivationFunctionType
AXX = mybir.AxisListType.X

P = 128
D = 1024
KD = D // P
SEQ, DEC = 1024, 32
T = SEQ + DEC
NT = SEQ // P + 1
W_A = W_B = 512
FT = W_A // P
CONV_W = 4
PAD = CONV_W - 1
LRU_C = 8.0
H_B = 4
DK = P
N_IN = 2 * W_A + 4 * W_B + 2 * H_B
HEADS, TOPK = 8, 16
GROUPS = P // DEC
TOPK_S = TOPK // GROUPS
SLOTS = (NT - 1) * TOPK + TOPK_S
DQ = 256
EPS = 1e-6
ZG = T // 3
XL = PAD + SEQ + PAD + DEC
UL = XL - PAD
LG = UL // 3
NEG = -1.0e30
NEG_MAX = -3.0e38
K_ROUTE, K_MIX, K_FIN = 14, 6, 4
EXP_MAX = 80.0
GELU_C = 0.044715
GELU_S = 2.0 * 0.7978845608028654
LOG1P = [1.0 / k for k in range(3, 19, 2)]

OUTS = [(1, SEQ, D), (1, DEC, D), (1, 1, W_A), (1, 1, PAD, W_A), (1, 1, H_B, DK, DK), (1, 1, H_B, DK),
        (1, 1, H_B), (1, 1, W_A), (1, 1, PAD, W_A), (1, 1, H_B, DK, DK), (1, 1, H_B, DK), (1, 1, H_B)]


def rows(t):
    return P if t < NT - 1 else DEC


def stream(t):
    return 0 if t < NT - 1 else 1


def build(nc, A, outs):
    with ExitStack() as ctx:
        def sb(name, shape, dt=F32):
            return ctx.enter_context(nc.sbuf_tensor(name, shape, dt))

        def sem(name):
            return ctx.enter_context(nc.semaphore(name))

        mod_dram = nc.dram_tensor("mod_dram", (2, 6 * D), F32, kind="Internal").ap()
        x1_dram = nc.dram_tensor("x1_dram", (T, D), F32, kind="Internal").ap()

        r_hT = sb("r_hT", [P, KD * T])
        r_qk = sb("r_qk", [P, NT * D])
        r_vo = sb("r_vo", [P, NT * (4 * 129 + 512)])
        r_yT = sb("r_yT", [P, KD * T])
        r_w = sb("r_w", [P, 12288])
        r_wq = sb("r_wq", [P, 4 * 516])
        ident = sb("ident", [P, P])
        ones = sb("ones", [P, P])
        mask = sb("mask", [P, P])
        seleye = sb("seleye", [H_B, H_B, P])
        wrd = sb("wrd", [P, FT, P])
        wid = sb("wid", [P, FT, P])
        kTt = sb("kTt", [P, 2, P])
        pos16 = sb("pos16", [P, TOPK])
        prm = sb("prm", [P, 552])
        gidx = sb("gidx", [P, NT * TOPK], I32)
        gate = sb("gate", [P, NT * TOPK])

        hT = r_hT[:, :].rearrange("p (k t) -> p k t", k=KD)
        xin = r_vo[:, 0:NT * D].rearrange("p (t d) -> p t d", t=NT)
        ada = r_w[:, :].rearrange("p (s k n) -> p s k n", s=3, k=KD)
        abias = r_yT[0:1, 0:1536].rearrange("p (s n) -> p s n", s=3)
        modrow = r_yT[0:2, 1536:2560].rearrange("p (s n) -> p s n", s=2)
        sq_junk = r_yT[:, 2560:3584]
        wblk = r_w[:, :].rearrange("p (s k n) -> p s k n", s=12, k=KD)
        qT = r_qk[:, 0:4 * T].rearrange("p (h t) -> p h t", h=H_B)
        kT = r_qk[:, 4 * T:8 * T].rearrange("p (h t) -> p h t", h=H_B)
        yT = r_yT[:, :].rearrange("p (k t) -> p k t", k=KD)
        lru = [r_vo[:, i * XL:(i + 1) * XL] for i in range(8)] + [r_yT[:, 4 * T + i * XL:4 * T + (i + 1) * XL] for i in range(3)]
        xpad, ga, uu = lru[0:2], lru[2:4], lru[4:6]
        rr, ii, aa, dd, pp = lru[6], lru[7], lru[8], lru[9], lru[10]
        wv = r_w[:, 4096:8192].rearrange("p (k n) -> p k n", k=KD)
        wo = r_w[:, 8192:12288].rearrange("p (k n) -> p k n", k=KD)
        vext = r_vo[:, 0:NT * 516].rearrange("p (t h e) -> p t h e", t=NT, h=H_B)
        og = r_vo[:, NT * 516:NT * 1028].rearrange("p (t n) -> p t n", t=NT)
        ra = [r_yT[0:8, (4 + i) * T:(5 + i) * T] for i in range(4)]
        zif, fro, aro, mro = ra[0], ra[1][0:H_B], ra[2][0:H_B], ra[3][0:H_B]
        negm = ra[1][0:H_B, 0:1024].rearrange("p (s h t) -> p s h t", s=2, h=H_B)
        wst, nmr, wkr = (r_w[0:H_B, i * T:(i + 1) * T] for i in range(3))
        hh = r_hT[:, 0:NT * 512].rearrange("p (t n) -> p t n", t=NT)
        o0 = NT * 512
        decay = [r_hT[:, o0 + i * 512:o0 + (i + 1) * 512].rearrange("p (h t) -> p h t", h=H_B) for i in range(2)]
        prob = [r_hT[:, o0 + 1024 + i * 512:o0 + 1536 + i * 512].rearrange("p (h t) -> p h t", h=H_B) for i in range(2)]
        kw = r_hT[:, o0 + 2048:o0 + 2560].rearrange("p (h t) -> p h t", h=H_B)
        nd = [r_hT[:, o0 + 2560 + i * 516:o0 + 3076 + i * 516].rearrange("p (h e) -> p h e", h=H_B) for i in range(2)]
        cst = r_wq[:, :].rearrange("p (b h e) -> p b h e", b=4, h=H_B)
        wout = r_w[:, 4096:12288].rearrange("p (k n) -> p k n", k=KD)
        xr = r_w[:, 0:4096].rearrange("p (s d) -> p s d", s=4)
        g1b, sh2b, a2b = (r_vo[:, i * 2048:(i + 1) * 2048].rearrange("p (s d) -> p s d", s=2) for i in range(3))
        n2b = r_vo[:, 6144:7168]
        h2 = r_qk[:, :].rearrange("p (t d) -> p t d", t=NT)
        h2T = hT
        wqh = r_wq[:, 0:2048].rearrange("p (k n) -> p k n", k=KD)
        uring = r_yT[:, 0:8192].rearrange("p (s d) -> p s d", s=8)
        vring = r_w[:, 4096:12288].rearrange("p (s d) -> p s d", s=8)
        acc = r_vo[:, 0:NT * D].rearrange("p (t d) -> p t d", t=NT)
        bt = r_w[:, 0:4096]
        bat = [0]

        def work(n):
            bat[0] += n
            return bt[:, bat[0] - n:bat[0]]

        diag = work(512).rearrange("p (s d) -> p s d", s=4)
        qts = work(256).rearrange("p (c t) -> p c t", c=2)
        qsq = work(256).rearrange("p (c t) -> p c t", c=2)
        swk, cand, cand2 = work(256), work(256), work(256)
        hot = [work(256).rearrange("p (a b) -> p a b", a=TOPK) for _ in range(2)]
        udump = [work(512).bitcast(BF16) for _ in range(2)]
        top, topf, sabf, e12 = work(32), work(32), work(32), work(32)
        topi, sab = work(32).bitcast(U32), work(32).bitcast(U32)
        sv, si = work(16), work(16).bitcast(U32)
        pexp, dots, gl, gl2, wgt = (work(TOPK) for _ in range(5))
        uidx, uidx_s, vidx, vidx_s = (work(n).bitcast(I32) for n in (TOPK, TOPK_S, TOPK, TOPK_S))
        qrt, qrs, nsv0, psm, prs, fss, frs = (work(1) for _ in range(7))
        gidx_t = gidx[:, :].rearrange("p (t j) -> p t j", t=NT)
        gate_t = gate[:, :].rearrange("p (t j) -> p t j", t=NT)
        h2T_t = h2T[:, :, 0:SEQ].rearrange("p k (t c) -> p k t c", c=P)
        def feat(a):
            return a.rearrange("p (k c) -> p k c", k=KD)

        g2b, fwb, x1s, fdump = (h2T_t[:, :, t, :] for t in range(4))
        g2s = h2T_t[0:DEC, :, 4, :]

        at = [0]

        def col(n):
            at[0] += n
            return prm[:, at[0] - n:at[0]]

        cT = col(16).rearrange("p (s k) -> p s k", s=2)
        ce = col(16).rearrange("p (s k) -> p s k", s=2)
        csil = col(16).rearrange("p (s k) -> p s k", s=2)
        n1T = col(8)
        modT = col(32).rearrange("p (a s k) -> p a s k", a=2, s=2)
        mul1 = col(16).rearrange("p (s k) -> p s k", s=2)
        binT = col(16)
        binq = col(4)
        bif = col(1)
        convw = col(16).rearrange("p (k f) -> p k f", k=CONV_W)
        convb, nbr, nbi, lam, lt1, lt2, c8, nc8 = (col(4) for _ in range(8))
        h0T = col(4)
        cv0 = col(12).rearrange("p (f r) -> p f r", f=FT)
        hl = col(8).rearrange("p (s f) -> p s f", s=2)
        cvn = col(24).rearrange("p (s f r) -> p s f r", s=2, f=FT)
        wif = col(64).rearrange("p (k n) -> p k n", k=KD)
        ssq = col(NT)
        rstd1 = col(NT)
        ssqh = col(36)
        rsth = col(36)
        mprev = col(NT)
        mend = col(2)
        mlast = col(NT)
        wcr = col(NT)
        wcd = col(36).rearrange("p (c h) -> p c h", c=NT)
        wcb = col(36).rearrange("p (c h) -> p c h", c=NT)
        den = col(4)
        rden = col(4)
        epsc = col(1)
        sel32 = col(DEC)
        ssq2 = col(NT)
        rstd2 = col(NT)
        assert at[0] <= 552, at[0]
        ra2 = sb("colsx", [P, NT * 12])
        colT = ra2[:, :].rearrange("p (t a h) -> p t a h", t=NT, a=3)
        nwb = r_qk[:, 8 * T:8 * T + W_B]
        bvo = [wrd[0:1, :, :].rearrange("p f n -> p (f n)"), wid[0:1, :, :].rearrange("p f n -> p (f n)")]
        kts = r_yT[:, 3584:3840]
        kwj = r_hT[:, 8200:8328]
        sq2 = r_vo[:, 7168:8192]

        ps = ctx.enter_context(nc.psum_tensor("ps", [P, 8, 512], F32))

        ld_c, ld_prm, ld_x, ld_modT = sem("ld_c"), sem("ld_prm"), sem("ld_x"), sem("ld_modT")
        ada_ld = [sem(f"ada_ld{i}") for i in range(3)]
        ada_mm, mod_ev = sem("ada_mm"), sem("mod_ev")
        mod_st = [sem(f"mod_st{i}") for i in range(2)]
        c_exp, c_silu = sem("c_exp"), sem("c_silu")
        consts, x_sq, x_rt, x_sc, x_tr, x_evd, x_eva, mul1_ready = (sem(n) for n in (
            "consts", "x_sq", "x_rt", "x_sc", "x_tr", "x_evd", "x_eva", "mul1_ready"))
        w_ld = [sem(f"w_ld{i}") for i in range(12)]
        vo_ld, wout_ld = [sem("v_ld"), sem("o_ld")], sem("wout_ld")
        z_mm, z_ev, lg_mm, lg_ev = (sem(n) for n in ("z_mm", "z_ev", "lg_mm", "lg_ev"))
        conv_done, rg_ready, lru_ac, lru_d3, lru_d4a, lru_bx, lru_scan, lru_y = (sem(n) for n in (
            "conv_done", "rg_ready", "lru_ac", "lru_d3", "lru_d4a", "lru_bx", "lru_scan", "lru_y"))
        lam_abs, lam_exp, c8_ready = sem("lam_abs"), sem("lam_exp"), sem("c8_ready")
        f_ld, f_abs, f_exp, row_ready, row_exp, row_tr, col_ready = (sem(n) for n in (
            "f_ld", "f_abs", "f_exp", "row_ready", "row_exp", "row_tr", "col_ready"))
        v_ones, og_ready = sem("v_ones"), sem("og_ready")
        st_ld = sem("st_ld")
        negm_ready, k_tr, kw_ready, s_mm, d_mm, d_exp, p_ready, c_mm, c_upd, n_mm, i_mm, n_ev, nd_done, h_ready, h_sq = (
            sem(n) for n in ("negm_ready", "k_tr", "kw_ready", "s_mm", "d_mm", "d_exp", "p_ready", "c_mm", "c_upd",
                             "n_mm", "i_mm", "n_ev", "nd_done", "h_ready", "h_sq"))
        h_rt, y_ready, y_tr, y_ev = sem("h_rt"), sem("y_ready"), sem("y_tr"), sem("y_ev")
        bc_ld, a2_ready = sem("bc_ld"), sem("a2_ready")
        xr_ld = [sem(f"xr_ld{i}") for i in range(4)]
        x1_st = [sem(f"x1_st{i}") for i in range(4)]
        o_mm, x1_ready, x1_sq, x1_rt, h2_ready, h2_tr, h2_ev = (sem(n) for n in (
            "o_mm", "x1_ready", "x1_sq", "x1_rt", "h2_ready", "h2_tr", "h2_ev"))
        kt_ld, kt_tr, kt_ready = sem("kt_ld"), sem("kt_tr"), sem("kt_ready")
        dve_step, act_step, pool_step = sem("dve_step"), sem("act_step"), sem("pool_step")
        out_st, bvo_ld = sem("out_st"), sem("bvo_ld")
        wq_ld, q_mm, q_sb, q_rt, r_mm, r_cp, p_in, p_exp, idx_ready, idx_cp = (sem(n) for n in (
            "wq_ld", "q_mm", "q_sb", "q_rt", "r_mm", "r_cp", "p_in", "p_exp", "idx_ready", "idx_cp"))
        u_ld = [sem(f"u_ld{j}") for j in range(8)]
        v_ld = [sem(f"v_ld{j}") for j in range(8)]
        u_free, v_free, g_in, g_exp, w_ready, dg_ready, acc_done = (sem(n) for n in (
            "u_free", "v_free", "g_in", "g_exp", "w_ready", "dg_ready", "acc_done"))
        route_step, mix_step, fin_step = sem("route_step"), sem("mix_step"), sem("fin_step")
        g2_ld, x1_ld, f_var, f_rt, y_out, y_st = (sem(n) for n in (
            "g2_ld", "x1_ld", "f_var", "f_rt", "y_out", "y_st"))
        pool_turn, pe_turn, dve_turn = sem("pool_turn"), sem("pe_turn"), sem("dve_turn")
        LAST = HEADS - 1
        N_STATE_STORES = 2 * (1 + FT + 1 + 2)
        n_out, n_prm = [0], [0]

        class Chain:

            def __init__(self, eng, s):
                self.eng, self.s, self.n, self.base = eng, s, 0, 0

            def link(self, ins):
                self.n += 1
                ins.then_inc(self.s, 1)
                self.eng.wait_ge(self.s, self.base + self.n)

        def number(h, t):
            return h * NT + t

        def slot0(h, t):
            return h * SLOTS + t * TOPK

        def first(t):
            return isinstance(t, int) and t == 0

        def slots(r):
            return TOPK if r == P else TOPK_S

        def landed(h, t, j):
            per_head = 2 * (NT - 1) + (1 if j % 8 < TOPK_S else 0)
            return h * (16 * per_head) + t * 32 + 16 * (j // 8 + 1)

        def each_step(eng, step):
            def tiles(h, last):
                fn = lambda *a: step(h, *a, last)
                fn(0, P, NT - 1, DEC, 2, P)
                with eng.Fori(0, NT - 4) as s:
                    fn(s + 1, P, s, P, s + 3, P)
                fn(NT - 3, P, NT - 4, P, NT - 1, DEC)
                fn(NT - 2, P, NT - 3, P, None if last else 0, P)
                fn(NT - 1, DEC, NT - 2, P, None if last else 1, P)

            with eng.Fori(0, LAST) as h:
                tiles(h, False)
            tiles(LAST, True)

        block = ctx.enter_context(nc.Block())

        lb = ["xa0", "ga0", "xa1", "G0", "ga1", "xa2", "q0", "G1", "ga2", "xa3", "q1", "G2", "ga3", "q2", "G3", "q3",
              "k0", "k1", "k2", "k3"]
        zblocks = [b for b in lb if b[0] != "G"]
        zcol = {"xa": 0, "ga": 4, "q": 8, "k": 12}

        def blk(b):
            return b[:-1], int(b[-1]), (zcol[b[:-1]] + int(b[-1]))

        def col_view(a, n):
            return a.rearrange("(j p) -> p j", p=P)

        @block.sync
        def _(sp):
            sp.dma_start(cT[:, 0, :], A["c_prompt"].rearrange("a (k p) -> p (a k)", p=P),
                         allow_slow_non_contiguous=True).then_inc(ld_c, 16)
            sp.dma_start(cT[:, 1, :], A["c_sample"].rearrange("a (k p) -> p (a k)", p=P),
                         allow_slow_non_contiguous=True).then_inc(ld_c, 16)
            ada_v = A["ada_w"][0].rearrange("(k p) n -> p k n", p=P)
            for b in range(12):
                if b >= 3:
                    sp.wait_ge(ada_mm, b - 2)
                sp.dma_start(ada[:, b % 3], ada_v[:, :, b * 512:(b + 1) * 512]).then_inc(ada_ld[b % 3], 16)
                sp.dma_start(abias[:, b % 3, :], A["ada_b"][:, b * 512:(b + 1) * 512]).then_inc(ada_ld[b % 3], 16)
            win_v = A["w_in"][0].rearrange("(k p) n -> p k n", p=P)
            for i, b in enumerate(zblocks):
                if i < 12:
                    sp.wait_ge(ada_mm, 10 + i // 4)
                else:
                    sp.wait_ge(z_mm, 3 * (i - 11))
                c = blk(b)[2] * P
                sp.dma_start(wblk[:, i % 12], win_v[:, :, c:c + P]).then_inc(w_ld[i % 12], 16)
            for n, dst in enumerate((wv, wo)):
                sp.wait_ge(z_mm, 3 * (8 + 4 * n))
                c = 2 * W_A + (2 + n) * W_B
                sp.dma_start(dst, win_v[:, :, c:c + W_B]).then_inc(vo_ld[n], 16)
            sp.wait_ge(z_mm, 51 + 2 * NT)
            sp.dma_start(wout, A["w_out"][0].rearrange("(k p) n -> p k n", p=P)).then_inc(wout_ld, 16)
            sp.wait_ge(col_ready, 2)
            xs = [A["x_prompt"][0, t * P:(t + 1) * P, :] for t in range(NT - 1)] + [A["x_sample"][0]]
            for t in range(NT):
                if t >= 4:
                    sp.wait_ge(x1_st[t % 4], 16 * (t // 4))
                    sp.wait_ge(x1_sq, t - 3)
                    sp.wait_ge(h2_ready, t - 3)
                sp.dma_start(xr[0:rows(t), t % 4, :], xs[t]).then_inc(xr_ld[t % 4], 16)
            wq_v = A["peer_wq"][0].rearrange("(k p) (h n) -> p k h n", p=P, h=HEADS)
            sp.wait_ge(i_mm, NT)
            sp.wait_ge(out_st, 16 * N_STATE_STORES)
            sp.dma_start(wqh, wq_v[:, :, 0, :]).then_inc(wq_ld, 16)
            with sp.Fori(1, HEADS) as h:
                sp.wait_ge(q_mm, h * NT)
                sp.dma_start(wqh, wq_v[:, :, h, :]).then_inc(wq_ld, 16)
            sp.wait_ge(q_mm, LAST * NT + 1)
            sp.dma_start(g2b, feat(mod_dram[0, 5 * D:6 * D].partition_broadcast(P))).then_inc(g2_ld, 16)
            sp.wait_ge(q_mm, LAST * NT + 2)
            sp.dma_start(fwb, feat(A["final_norm_w"].partition_broadcast(P))).then_inc(g2_ld, 16)
            for s in range(4):
                sp.wait_ge(x1_st[s], 16 * (3 if s == 0 else 2))
            x1_t = x1_dram[0:SEQ].rearrange("(t p) d -> t p d", p=P)
            y_t = outs[0][0].rearrange("(t p) d -> t p d", p=P)
            sp.wait_ge(q_mm, LAST * NT + 3)

            def finish(t, r, src, dst):
                sp.dma_start(x1s[0:r], feat(src)).then_inc(x1_ld, 16)
                sp.wait_ge(y_out, t + 1)
                sp.dma_start(dst, acc[0:r, t, :]).then_inc(y_st, 16)

            finish(0, P, x1_t[0], y_t[0])
            sp.wait_ge(q_mm, LAST * NT + 5)
            sp.dma_start(g2s, feat(mod_dram[1, 5 * D:6 * D].partition_broadcast(DEC))).then_inc(g2_ld, 16)
            with sp.Fori(1, NT - 1) as t:
                finish(t, P, x1_t[t], y_t[t])
            finish(NT - 1, DEC, x1_dram[SEQ:T], outs[1][0])
            sp.wait_ge(y_st, 16 * NT)

        @block.gpsimd
        def _(pool):
            ch = Chain(pool, pool_step)
            for m, v in ((ident[:, :], 0.0), (mask[:, :], 0.0), (seleye[:, :, :], 0.0), (wrd[:, :, :], 0.0),
                         (wid[:, :, :], 0.0), (ones[:, :], 1.0), (ssq, 1.0), (ssqh, 1.0), (ssq2, 1.0)):
                ch.link(nc.gpsimd.memset(m, v))
            ch.link(nc.gpsimd.affine_select(out=ident[:, :], in_=ident[:, :], compare_op=ALU.not_equal, fill=1.0, base=0,
                                            pattern=[[-1, P]], channel_multiplier=1))
            ch.link(nc.gpsimd.affine_select(out=mask[:, :], in_=mask[:, :], compare_op=ALU.is_ge, fill=NEG, base=0,
                                            pattern=[[1, P]], channel_multiplier=-1))
            ch.link(nc.gpsimd.affine_select(out=seleye[:, :, :], in_=seleye[:, :, :], compare_op=ALU.not_equal, fill=1.0,
                                            base=0, pattern=[[-1, H_B], [0, P]], channel_multiplier=1))
            nc.gpsimd.iota(pos16[:, :], pattern=[[1, TOPK]], base=0, channel_multiplier=0,
                           allow_small_or_imprecise_dtypes=True).then_inc(consts, 1)

            def load(dst, src):
                n_prm[0] += 16
                pool.dma_start(dst, src, allow_slow_non_contiguous=True).then_inc(ld_prm, 16)

            load(n1T, col_view(A["norm1_w"][0], 8))
            load(binT, col_view(A["b_in"][0, 0:2048], 16))
            load(bif[0:8], A["b_in"][0, 3072:3080].rearrange("(p j) -> p j", j=1))
            load(convw, A["conv_w"][0].rearrange("k (f p) -> p k f", p=P))
            for dst, nm in ((convb, "conv_b"), (nbr, "lru_br"), (nbi, "lru_bi"), (lam, "lru_lambda")):
                load(dst, col_view(A[nm][0], 4))
            load(h0T, col_view(A["state_lru_h"][0, 0], 4))
            for f in range(FT):
                load(cv0[:, f, :], A["state_lru_conv"][0, 0, :, f * P:(f + 1) * P].rearrange("r p -> p r"))
            for half in range(2):
                hs = slice(64 * half, 64 * half + 64)
                load(wrd[hs, :, hs], A["lru_wr"][0, half::2].rearrange("n c d -> c n d"))
                load(wid[hs, :, hs], A["lru_wi"][0, half::2].rearrange("n c d -> c n d"))
            load(wif, A["w_in"][0, :, 3072:3080].rearrange("(k p) n -> p k n", p=P))
            load(nwb[:, :], A["mlstm_norm_w"][0].partition_broadcast(P))
            load(mprev[0:H_B, NT - 1:NT], A["state_mlstm_m"][0, 0].rearrange("(p j) -> p j", j=1))
            for b in range(12):
                pool.wait_ge(mod_ev, b + 1)
                pool.dma_start(mod_dram[:, b * 512:(b + 1) * 512], modrow[:, b % 2, :]).then_inc(mod_st[b % 2], 16)
                if b == 3:
                    for s in range(2):
                        pool.wait_ge(mod_st[s], 32)
                    for a in range(2):
                        for s in range(2):
                            pool.dma_start(modT[:, a, s, :], col_view(mod_dram[s, a * D:(a + 1) * D], 8),
                                           allow_slow_non_contiguous=True).then_inc(ld_modT, 16)
            for s in range(2):
                pool.wait_ge(mod_st[s], 96)
            pool.wait_ge(z_ev, 51)
            pool.dma_start(fro, zif[H_B:2 * H_B, :]).then_inc(f_ld, 16)
            pool.wait_ge(lg_mm, 24)
            for n in range(2):
                pool.dma_start(bvo[n], A["b_in"][:, 2048 + n * W_B:2048 + (n + 1) * W_B]).then_inc(bvo_ld, 16)
            pool.dma_start(cst[:, 2, :, 0:DK], A["state_mlstm_C"][0, 0].rearrange("h k v -> k h v")).then_inc(st_ld, 16)
            pool.dma_start(cst[:, 2, :, DK:DK + 1], A["state_mlstm_n"][0, 0].rearrange("h (k j) -> k h j", j=1),
                           allow_slow_non_contiguous=True).then_inc(st_ld, 16)

            def store(dst, src):
                n_out[0] += 16
                pool.dma_start(dst, src, allow_slow_non_contiguous=True).then_inc(out_st, 16)

            pool.wait_ge(lru_y, 2 * FT)
            for s in range(2):
                store(outs[2 + 5 * s][0, 0].rearrange("(f p) -> p f", p=P), hl[:, s, :])
                for f in range(FT):
                    store(outs[3 + 5 * s][0, 0, :, f * P:(f + 1) * P].rearrange("r p -> p r"), cvn[:, s, f, :])
            pool.wait_ge(row_ready, 1)
            for s in range(2):
                store(outs[6 + 5 * s][0, 0].rearrange("(p j) -> p j", j=1), mend[0:H_B, s:s + 1])
            for s, b in ((0, 0), (1, 3)):
                pool.wait_ge(c_upd, NT - 1 + s)
                store(outs[4 + 5 * s][0, 0].rearrange("h k v -> k h v"), cst[:, b, :, 0:DK])
                store(outs[5 + 5 * s][0, 0].rearrange("h (k j) -> k h j", j=1), cst[:, b, :, DK:DK + 1])
            pool.wait_ge(y_tr, NT)
            for dst, c in ((g1b, 2), (sh2b, 3), (a2b, 4)):
                for s in range(2):
                    n = P if s == 0 else DEC
                    pool.dma_start(dst[0:n, s, :], mod_dram[s, c * D:(c + 1) * D].partition_broadcast(n)).then_inc(bc_ld, 16)
            pool.dma_start(n2b, A["norm2_w"][0].partition_broadcast(P)).then_inc(bc_ld, 16)
            for t in range(NT):
                pool.wait_ge(x1_ready, t + 1)
                pool.dma_start(x1_dram[t * P:t * P + rows(t), :], xr[0:rows(t), t % 4, :]).then_inc(x1_st[t % 4], 16)
            pool.wait_ge(o_mm, NT)
            for s in range(4):
                pool.wait_ge(x1_st[s], 16 * (3 if s == 0 else 2))
            eu, ev = A["peer_u"][0], A["peer_v"][0]

            def hold():
                pool.sem_inc(pool_turn, 1)

            def gather(h, t, r, j, idx, table, ring, done, ld):
                former = 5 if first(t) and j < TOPK_S else 1
                if not first(t) or j < TOPK_S or j >= 8:
                    pool.wait_ge(done, slot0(h, t) + (j + former))
                    hold()
                pool.indirect_dma_start(ring[:, j % 8, :], None, table, bass.IndirectOffsetOnAxis(idx[:, j:j + 1], 0))\
                    .then_inc(ld[j % 8], 16)

            def take_rows(h, t, r, copies, full, sample, done):
                k = slots(r)
                dst = full if r == P else sample
                pool.wait_ge(idx_ready, number(h, t) + 1)
                if r == P:
                    pool.wait_ge(done, slot0(h, t) + (4 if first(t) else 8))
                hold()
                nc.gpsimd.tensor_copy(dst[:, 0:k], gidx_t[:, t, 0:k]).then_inc(idx_cp, 1)
                pool.wait_ge(idx_cp, number(h, t) * 2 + copies)
                hold()
                return dst

            def u_rows(h, t, r):
                idx = take_rows(h, t, r, 1, uidx, uidx_s, u_free)
                return [lambda j=j: gather(h, t, r, j, idx, eu, uring, u_free, u_ld) for j in range(slots(r))]

            def gathers(h, t, r, following):
                idx = take_rows(h, t, r, 2, vidx, vidx_s, v_free)
                k = slots(r)
                u = None
                for j in range(k):
                    gather(h, t, r, j, idx, ev, vring, v_free, v_ld)
                    if j == min(k, 8) - 1 and following:
                        u = u_rows(*following)
                    elif j >= 8 and u:
                        u.pop(0)()
                for row in u or []:
                    row()

            for row in u_rows(0, 0, P):
                row()

            def tiles(h, after):
                gathers(h, 0, P, (h, 1, P))
                with pool.Fori(0, NT - 3) as s:
                    gathers(h, s + 1, P, (h, s + 2, P))
                gathers(h, NT - 2, P, (h, NT - 1, DEC))
                gathers(h, NT - 1, DEC, after)

            with pool.Fori(0, LAST) as h:
                tiles(h, (h + 1, 0, P))
            tiles(LAST, None)
            pool.wait_ge(out_st, n_out[0])

        @block.tensor
        def _(pe):
            def ada_block(b):
                pe.wait_ge(ada_ld[b % 3], 32 * (b // 3 + 1))
                if b >= 2:
                    pe.wait_ge(mod_ev, b - 1)
                out = ps[0:2, b % 2, :]
                for k in range(KD):
                    nc.tensor.matmul(out, csil[:, :, k], ada[:, b % 3, k, :], start=k == 0, stop=False)
                nc.tensor.matmul(out, ones[0:1, 0:2], abias[:, b % 3, :], start=False, stop=True).then_inc(ada_mm, 1)

            pe.wait_ge(consts, 1)
            pe.wait_ge(c_silu, 1)
            for b in range(4):
                ada_block(b)
            pe.wait_ge(kt_ld, 32)
            for i in range(2):
                m = nc.tensor.transpose(ps[:, 6, i * P:(i + 1) * P], kts[:, i * P:(i + 1) * P], ident[:, :])
            m.then_inc(kt_tr, 1)
            for b in range(4, 6):
                ada_block(b)
            for t in range(NT):
                r = rows(t)
                pe.wait_ge(x_sc, t + 1)
                for j in range(2):
                    if t >= 2:
                        pe.wait_ge((x_evd, x_eva)[j], t - 1)
                    for k in range(4):
                        m = nc.tensor.transpose(ps[:, 2 + 2 * (t % 2) + j, k * P:k * P + r],
                                                xin[0:r, t, (4 * j + k) * P:(4 * j + k + 1) * P], ident[0:r, 0:r])
                    m.then_inc(x_tr, 1)
            for b in range(6, 12):
                ada_block(b)
            pe.wait_ge(mod_ev, 12)
            pe.wait_ge(x_evd, NT)
            pe.wait_ge(x_eva, NT)
            unit = [0]

            def z_bank():
                u = unit[0]
                unit[0] += 1
                if u >= 4:
                    pe.wait_ge(z_ev, u - 3)
                return u % 4

            gunit = [0]
            pe.wait_ge(kt_ready, 1)
            nblk = 0
            for b in lb:
                if b[0] == "G":
                    f = int(b[1])
                    pe.wait_ge(conv_done, f + 1)
                    if f == 0:
                        pe.wait_ge(ld_prm, n_prm[0])
                    for w in (wrd, wid):
                        for g in range(3):
                            if gunit[0] >= 4:
                                pe.wait_ge(lg_ev, gunit[0] - 3)
                            nc.tensor.matmul(ps[:, 4 + gunit[0] % 4, 0:LG], w[:, f, :], uu[f % 2][:, g * LG:(g + 1) * LG],
                                             start=True, stop=True).then_inc(lg_mm, 1)
                            gunit[0] += 1
                    continue
                pe.wait_ge(w_ld[nblk % 12], 16 * (nblk // 12 + 1))
                for g in range(3):
                    bank = z_bank()
                    for k in range(KD):
                        m = nc.tensor.matmul(ps[:, bank, 0:ZG], wblk[:, nblk % 12, k, :], hT[:, k, g * ZG:(g + 1) * ZG],
                                             start=k == 0, stop=k == KD - 1)
                    m.then_inc(z_mm, 1)
                nblk += 1
            for g in range(3):
                bank = z_bank()
                for k in range(KD):
                    m = nc.tensor.matmul(ps[0:8, bank, 0:ZG], wif[:, k, :], hT[:, k, g * ZG:(g + 1) * ZG],
                                         start=k == 0, stop=k == KD - 1)
                m.then_inc(z_mm, 1)
            pe.wait_ge(bvo_ld, 32)
            for t in range(NT):
                r = rows(t)
                for n, w in enumerate((wv, wo)):
                    bank = z_bank()
                    if t == 0:
                        pe.wait_ge(vo_ld[n], 16)
                    for k in range(KD):
                        nc.tensor.matmul(ps[0:r, bank, :], hT[:, k, t * P:t * P + r], w[:, k, :], start=k == 0, stop=False)
                    nc.tensor.matmul(ps[0:r, bank, :], ones[0:1, 0:r], bvo[n],
                                     start=False, stop=True).then_inc(z_mm, 1)
            pe.wait_ge(row_exp, 1)
            pe.wait_ge(lg_ev, 24)
            for t in range(NT):
                r = rows(t)
                for a, row in enumerate((wst, nmr, wkr)):
                    nc.tensor.transpose(ps[0:r, 4, (t * 3 + a) * 4:(t * 3 + a) * 4 + 4], row[:, t * P:t * P + r],
                                        ident[0:H_B, 0:H_B])
            nc.tensor.matmul(ps[:, 4, 128:164], ones[0:H_B, :], wcd[0:H_B], start=True, stop=True).then_inc(row_tr, 1)
            pe.wait_ge(z_ev, 51 + 2 * NT)
            pe.wait_ge(col_ready, 2)

            def front(t):
                r, cs = rows(t), slice(t * P, t * P + rows(t))
                if t >= 1:
                    pe.wait_ge(p_ready, t)
                for h in range(H_B):
                    m = nc.tensor.transpose(ps[0:r, 0, h * P:(h + 1) * P], kT[:, h, cs], ident[:, :])
                m.then_inc(k_tr, 1)
                if t >= 1:
                    pe.wait_ge(d_exp, t)
                pe.wait_ge(negm_ready, t + 1)
                dst = ps[0:r, 1, :].rearrange("p (h t) -> p h t", h=H_B)[:, :, 0:r]
                nc.tensor.matmul(dst, ident[0:r, 0:r], mask[0:r, 0:r].unsqueeze(1).broadcast_to([r, H_B, r]),
                                 start=True, stop=False)
                nc.tensor.matmul(dst, aro[:, cs], seleye[:, :, 0:r], start=False, stop=False)
                nc.tensor.matmul(dst, ones[0:H_B, 0:r], negm[:, t % 2, :, 0:r], start=False, stop=True).then_inc(d_mm, 1)
                pe.wait_ge(kw_ready, t + 1)
                for h in range(H_B):
                    m = nc.tensor.matmul(ps[0:r, 0, h * P:h * P + r], kT[:, h, cs], qT[:, h, cs], start=True, stop=True)
                m.then_inc(s_mm, 1)
                if t >= 1:
                    pe.wait_ge(c_upd, t)
                for h in range(H_B):
                    m = nc.tensor.matmul(ps[:, 6 + h // 2, (h % 2) * 129:(h % 2) * 129 + 129], kw[0:r, h, :], vext[0:r, t, h, :],
                                         start=True, stop=True)
                m.then_inc(c_mm, 1)

            def back(t):
                r, cs = rows(t), slice(t * P, t * P + rows(t))
                if t >= 1:
                    pe.wait_ge(n_ev, t)
                    pe.wait_ge(nd_done, t)
                pe.wait_ge(p_ready, t + 1)
                for h in range(H_B):
                    m = nc.tensor.matmul(ps[0:r, 2 + h // 2, (h % 2) * 129:(h % 2) * 129 + 129], prob[t % 2][0:r, h, 0:r],
                                         vext[0:r, t, h, :], start=True, stop=True)
                m.then_inc(n_mm, 1)
                pe.wait_ge(c_upd, t) if t >= 1 else None
                if t == NT - 1:
                    pe.wait_ge(st_ld, 32)
                src = t % 2 if t < NT - 1 else 2
                for h in range(H_B):
                    m = nc.tensor.matmul(ps[0:r, 4 + h // 2, (h % 2) * 129:(h % 2) * 129 + 129], qT[:, h, cs], cst[:, src, h, :],
                                         start=True, stop=True)
                m.then_inc(i_mm, 1)

            front(0)
            for t in range(NT):
                if t + 1 < NT:
                    front(t + 1)
                back(t)
            pe.wait_ge(n_ev, NT)
            pe.wait_ge(p_ready, NT)
            pe.wait_ge(d_exp, NT)
            for t in range(NT):
                r = rows(t)
                pe.wait_ge(y_ready, t + 1)
                if t >= 2:
                    pe.wait_ge(y_ev, t - 1)
                for j in range(4):
                    m = nc.tensor.transpose(ps[:, t % 2, j * P:j * P + r], og[0:r, t, j * P:(j + 1) * P], ident[0:r, 0:r])
                m.then_inc(y_tr, 1)
            pe.wait_ge(wout_ld, 16)
            pe.wait_ge(y_ev, NT)
            pe.wait_ge(c_upd, NT)

            def project(t):
                r = rows(t)
                if t >= 2:
                    pe.wait_ge(x1_ready, t - 1)
                for c in range(2):
                    for k in range(KD):
                        m = nc.tensor.matmul(ps[0:r, 2 * (t % 2) + c, :], yT[:, k, t * P:t * P + r],
                                             wout[:, k, c * 512:(c + 1) * 512], start=k == 0, stop=k == KD - 1)
                m.then_inc(o_mm, 1)

            def turn_h2(t):
                r = rows(t)
                pe.wait_ge(h2_ready, t + 1)
                if t >= 2:
                    pe.wait_ge(h2_ev, t - 1)
                for k in range(KD):
                    m = nc.tensor.transpose(ps[:, 4 + 2 * (t % 2) + k // 4, (k % 4) * P:(k % 4) * P + r],
                                            h2[0:r, t, k * P:(k + 1) * P], ident[0:r, 0:r])
                m.then_inc(h2_tr, 1)

            for t in range(NT):
                project(t)
                if t >= 1:
                    turn_h2(t - 1)
            turn_h2(NT - 1)
            pe.wait_ge(h2_ev, NT)
            pe.wait_ge(x1_ready, NT)

            def hold():
                pe.sem_inc(pe_turn, 1)

            def route(t, m, r):
                pe.wait_ge(q_sb, m + 1)
                for c in range(2):
                    for k in range(KD):
                        rhs = h2T_t[:, k, t, :] if r == P else h2T[:, k, SEQ:T]
                        mm = nc.tensor.matmul(ps[:, 4, c * P:c * P + r], wqh[:, k, c * P:(c + 1) * P], rhs,
                                              start=k == 0, stop=k == KD - 1)
                mm.then_inc(q_mm, 1)
                pe.wait_ge(q_sb, m + 2)
                pe.wait_ge(r_cp, m + 1)
                hold()
                for c in range(2):
                    nc.tensor.matmul(ps[0:r, 5, c * P:(c + 1) * P], qts[:, c, 0:r], kTt[:, c, :], start=True, stop=True)
                for c in range(2):
                    mm = nc.tensor.matmul(ps[0:r, 6, 0:1], qsq[:, c, 0:r], ones[:, 0:1], start=c == 0, stop=c == 1)
                mm.then_inc(r_mm, 1)

            def mix(h, t, r):
                pe.wait_ge(acc_done, number(h, t) + 1)
                k = slots(r)
                for j in range(k):
                    pe.wait_ge(dg_ready, slot0(h, t) + (j + 1))
                    pe.wait_ge(v_ld[j % 8], landed(h, t, j))
                    hold()
                    for c in range(2):
                        mm = nc.tensor.matmul(ps[0:r, c, :], diag[:, j % 4, 0:r], vring[:, j % 8, c * 512:(c + 1) * 512],
                                              start=j == 0, stop=j == k - 1)
                    mm.then_inc(v_free, 1)

            pe.sem_inc(v_free, 8)
            pe.wait_ge(wq_ld, 16)
            route(0, 0, P)
            route(1, 1, P)

            def step(h, t, r, tp, rp, ta, ra, last):
                if ta is not None:
                    if first(ta):
                        pe.wait_ge(wq_ld, h * 16 + 32)
                        hold()
                    route(ta, number(h, t) + 2, ra)
                mix(h, t, r)

            each_step(pe, step)

        @block.scalar
        def _(act):
            ch = Chain(act, act_step)
            for t in range(NT - 1):
                act.dma_start(xin[:, t, :], A["x_prompt"][0, t * P:(t + 1) * P, :]).then_inc(ld_x, 16)
            act.dma_start(xin[0:DEC, NT - 1, :], A["x_sample"][0]).then_inc(ld_x, 16)
            for i, nm in enumerate(("peer_k1", "peer_k2")):
                act.dma_start(kts[:, i * P:(i + 1) * P], A[nm][0]).then_inc(kt_ld, 16)
            act.wait_ge(ld_c, 32)
            nc.scalar.activation(ce, cT, ACT.Exp, scale=-1.0).then_inc(c_exp, 1)
            act.wait_ge(ld_x, 16 * NT)
            act.wait_ge(consts, 1)
            for t in range(NT):
                r = rows(t)
                if t:
                    act.wait_ge(x_sq, t)
                nc.scalar.activation(sq_junk[0:r], xin[0:r, t, :], ACT.Square, accum_out=ssq[0:r, t:t + 1]).then_inc(x_sq, 1)
            act.wait_ge(x_sq, NT + 1)
            nc.scalar.activation(ssq, ssq, ACT.Sqrt).then_inc(x_rt, 1)
            act.wait_ge(kt_tr, 1)
            nc.scalar.activation(kTt[:, :, :], ps[:, 6, 0:256].rearrange("p (c k) -> p c k", c=2), ACT.Copy).then_inc(kt_ready, 1)
            act.wait_ge(mul1_ready, 1)
            for t in range(NT):
                r = rows(t)
                act.wait_ge(x_tr, 2 * t + 2)
                s = stream(t)
                for k in range(4):
                    m = nc.scalar.activation(hT[:, 4 + k, t * P:t * P + r], ps[:, 3 + 2 * (t % 2), k * P:k * P + r], ACT.Identity,
                                             scale=mul1[:, s, 4 + k:5 + k], bias=modT[:, 0, s, 4 + k:5 + k])
                m.then_inc(x_eva, 1)
            act.wait_ge(lam_abs, 1)
            nc.scalar.activation(lt1, lt1, ACT.Exp, scale=-1.0).then_inc(lam_exp, 1)
            act.wait_ge(c8_ready, 1)
            unit = 0

            def evac_z(b):
                nonlocal unit
                kind, j, cb = blk(b)
                if kind == "xa":
                    dst, off = xpad[j % 2], PAD
                    if j >= 2:
                        act.wait_ge(conv_done, j - 1)
                elif kind == "ga":
                    dst, off = ga[j % 2], 0
                    if j >= 2:
                        act.wait_ge(lru_y, 2 * (j - 1))
                else:
                    dst, off = (qT if kind == "q" else kT)[:, j, :], 0
                gap = PAD if kind in ("xa", "ga") else 0
                scale, bias = (DK ** -0.5, binq[:, j:j + 1]) if kind == "q" else (1.0, binT[:, cb:cb + 1])
                for g in range(3):
                    act.wait_ge(z_mm, unit + 1)
                    c0 = g * ZG
                    n = min(ZG, SEQ - c0)
                    m = nc.scalar.activation(dst[:, off + c0:off + c0 + n], ps[:, unit % 4, 0:n], ACT.Identity, scale=scale, bias=bias)
                    if n < ZG:
                        m = nc.scalar.activation(dst[:, off + SEQ + gap:off + gap + T], ps[:, unit % 4, n:ZG], ACT.Identity,
                                                 scale=scale, bias=bias)
                    m.then_inc(z_ev, 1)
                    unit += 1

            def gates(f):
                if f:
                    act.wait_ge(lru_scan, f)
                for w, (dst, bias) in enumerate(((rr, nbr), (ii, nbi))):
                    for g in range(3):
                        v = f * 6 + w * 3 + g
                        act.wait_ge(lg_mm, v + 1)
                        nc.scalar.activation(dst[:, g * LG:(g + 1) * LG], ps[:, 4 + v % 4, 0:LG], ACT.Exp, scale=-1.0,
                                             bias=bias[:, f:f + 1]).then_inc(lg_ev, 1)

            def decays(f):
                act.wait_ge(rg_ready, f + 1)
                if f:
                    act.wait_ge(lru_scan, f)
                ch.link(nc.scalar.activation(aa[:, 0:UL], rr[:, 0:UL], ACT.Exp, scale=nc8[:, f:f + 1]))
                nc.scalar.activation(rr[:, 0:UL], rr[:, 0:UL], ACT.Tanh, scale=c8[:, f:f + 1]).then_inc(lru_ac, 1)

            def roots(f):
                act.wait_ge(lru_d3, f + 1)
                nc.scalar.activation(pp[:, 0:UL], pp[:, 0:UL], ACT.Exp, scale=-GELU_S).then_inc(lru_d4a, 1)
                nc.scalar.activation(dd[:, 0:UL], dd[:, 0:UL], ACT.Sqrt).then_inc(lru_d4a, 1)

            after = {"xa1": [], "G0": [(gates, 0)], "ga1": [(decays, 0)], "xa2": [(roots, 0)], "G1": [(gates, 1)],
                     "ga2": [(decays, 1)], "xa3": [(roots, 1)], "G2": [(gates, 2)], "ga3": [(decays, 2)], "q2": [(roots, 2)],
                     "G3": [(gates, 3)], "q3": [(decays, 3)], "k0": [(roots, 3)]}
            for b in lb:
                if b[0] != "G":
                    evac_z(b)
                for fn, f in after.get(b, []):
                    fn(f)
            act.wait_ge(lru_y, 2 * FT)
            for g in range(3):
                act.wait_ge(z_mm, unit + 1)
                nc.scalar.activation(zif[:, g * ZG:(g + 1) * ZG], ps[0:8, unit % 4, 0:ZG], ACT.Identity,
                                     bias=bif[0:8]).then_inc(z_ev, 1)
                unit += 1

            def evac_vo(t):
                nonlocal unit
                r = rows(t)
                act.wait_ge(z_mm, unit + 1)
                nc.scalar.activation(vext[0:r, t, :, 0:DK], ps[0:r, unit % 4, :].rearrange("p (h e) -> p h e", h=H_B),
                                     ACT.Copy).then_inc(z_ev, 1)
                act.wait_ge(z_mm, unit + 2)
                nc.scalar.activation(og[0:r, t, :], ps[0:r, (unit + 1) % 4, :], ACT.Exp, scale=-1.0).then_inc(z_ev, 1)
                unit += 2

            for t in range(NT):
                evac_vo(t)
                if t == 2:
                    act.wait_ge(f_abs, 1)
                    nc.scalar.activation(nmr, wst, ACT.Exp, scale=-1.0).then_inc(f_exp, 1)
                if t == 6:
                    act.wait_ge(row_ready, 1)
                    for w in (wst, nmr, wkr):
                        ch.link(nc.scalar.activation(w, w, ACT.Exp))
                    nc.scalar.activation(wcr[0:H_B], wcr[0:H_B], ACT.Exp).then_inc(f_exp, 1)
            for t in range(NT):
                r = rows(t)

                def decay_exp(t):
                    r = rows(t)
                    act.wait_ge(d_mm, t + 1)
                    if t >= 2:
                        act.wait_ge(p_ready, t - 1)
                    nc.scalar.activation(decay[t % 2][0:r, :, 0:r], ps[0:r, 1, :].rearrange("p (h t) -> p h t", h=H_B)[:, :, 0:r],
                                         ACT.Exp).then_inc(d_exp, 1)
                if t == 0:
                    decay_exp(0)
                if t + 1 < NT:
                    decay_exp(t + 1)
                act.wait_ge(n_mm, t + 1)
                if t >= 2:
                    act.wait_ge(h_ready, t - 1)
                for b in range(2):
                    m = nc.scalar.activation(nd[t % 2][0:r, 2 * b:2 * b + 2, :],
                                             ps[0:r, 2 + b, 0:258].rearrange("p (h e) -> p h e", h=2), ACT.Copy)
                m.then_inc(n_ev, 1)
                act.wait_ge(h_ready, t + 1)
                for h in range(H_B):
                    if t or h:
                        act.wait_ge(h_sq, 4 * t + h)
                    m = nc.scalar.activation(kwj[0:r], hh[0:r, t, h * P:(h + 1) * P], ACT.Square,
                                             accum_out=ssqh[0:r, 4 * t + h:4 * t + h + 1]).then_inc(h_sq, 1)
            act.wait_ge(h_rt, 1)
            nc.scalar.activation(ssqh, ssqh, ACT.Sqrt).then_inc(h_rt, 1)
            for t in range(NT):
                r = rows(t)
                act.wait_ge(y_tr, t + 1)
                nc.scalar.activation(yT[:, 4:8, t * P:t * P + r],
                                     ps[:, t % 2, :].rearrange("p (j t) -> p j t", j=4)[:, :, 0:r], ACT.Copy).then_inc(y_ev, 1)

            def turn(t):
                r = rows(t)
                act.wait_ge(h2_tr, t + 1)
                for j in range(2):
                    m = nc.scalar.activation(h2T[:, 4 * j:4 * j + 4, t * P:t * P + r],
                                             ps[:, 4 + 2 * (t % 2) + j, :].rearrange("p (k t) -> p k t", k=4)[:, :, 0:r], ACT.Copy)
                m.then_inc(h2_ev, 1)

            for t in range(NT):
                r = rows(t)
                act.wait_ge(x1_ready, t + 1)
                if t >= 1:
                    act.wait_ge(x1_sq, t)
                nc.scalar.activation(sq2[0:r], xr[0:r, t % 4, :], ACT.Square, accum_out=ssq2[0:r, t:t + 1]).then_inc(x1_sq, 1)
                act.wait_ge(x1_rt, 2 * t + 1)
                nc.scalar.activation(rstd2[0:r, t:t + 1], rstd2[0:r, t:t + 1], ACT.Sqrt).then_inc(x1_rt, 1)
                if t >= 1:
                    turn(t - 1)
            turn(NT - 1)
            for s in range(4):
                act.wait_ge(x1_st[s], 16 * (3 if s == 0 else 2))
            act.wait_ge(h2_ready, NT)

            def query(m, r):
                act.wait_ge(q_mm, m + 1)
                act.wait_ge(r_mm, m + 1)
                for dst, fn in ((qts, ACT.Copy), (qsq, ACT.Square)):
                    last = nc.scalar.activation(dst[:, :, 0:r], ps[:, 4, 0:256].rearrange("p (c t) -> p c t", c=2)[:, :, 0:r], fn)
                last.then_inc(q_sb, 1)
                act.wait_ge(r_mm, m + 2)
                act.wait_ge(r_cp, m + 1)
                nc.scalar.activation(qrt[0:r], ps[0:r, 6, 0:1], ACT.Sqrt, scale=1.0 / DQ, bias=epsc[0:r]).then_inc(q_rt, 1)

            def softmax(m, r):
                act.wait_ge(p_in, m + 2)
                nc.scalar.activation(pexp[0:r], sv[0:r], ACT.Exp, scale=qrs[0:r], bias=nsv0[0:r],
                                     accum_out=psm[0:r]).then_inc(p_exp, 1)

            def weights(h, t, r, between):
                n, k = number(h, t), slots(r)
                act.wait_ge(g_in, n + 1)
                nc.scalar.activation(gl2[:, 0:k], gl[:, 0:k], ACT.Exp, scale=-GELU_S).then_inc(g_exp, 1)
                act.wait_ge(w_ready, n + 1)
                for j in range(k):
                    act.wait_ge(v_free, slot0(h, t) + (j + 5))
                    nc.scalar.activation(diag[:, j % 4, 0:r], (ident if r == P else sel32)[:, 0:r], ACT.Copy,
                                         scale=wgt[:, j:j + 1]).then_inc(dg_ready, 1)
                    if j in between:
                        between[j]()

            def final_root(t):
                act.wait_ge(f_var, t + 1)
                nc.scalar.activation(frs, frs, ACT.Sqrt).then_inc(f_rt, 1)

            act.sem_inc(q_sb, 1)
            act.sem_inc(r_mm, 1)
            for t in range(2):
                query(t, P)
                softmax(t, P)

            def step(h, t, r, tp, rp, ta, ra, last):
                m, between = number(h, t) + 2, {}
                if ta is not None:
                    query(m, ra)
                    between[slots(r) // 2 - 1] = lambda: softmax(m, ra)
                if last and not first(t):
                    between[slots(r) - 3] = lambda: final_root(tp)
                weights(h, t, r, between)

            each_step(act, step)
            final_root(NT - 1)

        @block.vector
        def _(dve):
            V = nc.vector
            ch = Chain(dve, dve_step)
            link = ch.link
            dve.wait_ge(c_exp, 1)
            link(V.tensor_scalar(ce, ce, 1.0, None, ALU.add))
            link(V.reciprocal(ce, ce))
            V.tensor_tensor(csil, cT, ce, ALU.mult).then_inc(c_silu, 1)
            for b in range(4):
                dve.wait_ge(ada_mm, b + 1)
                if b >= 2:
                    dve.wait_ge(mod_st[b % 2], 16 * (b // 2))
                V.tensor_copy(modrow[:, b % 2, :], ps[0:2, b % 2, :]).then_inc(mod_ev, 1)
            dve.wait_ge(x_sq, NT)
            V.tensor_scalar(ssq, ssq, 1.0 / D, EPS, ALU.mult, ALU.add).then_inc(x_sq, 1)
            dve.wait_ge(x_rt, 1)
            link(V.reciprocal(rstd1, ssq))
            for t in range(NT):
                r = rows(t)
                V.tensor_scalar(xin[0:r, t, :], xin[0:r, t, :], rstd1[0:r, t:t + 1], None, ALU.mult).then_inc(x_sc, 1)
            dve.wait_ge(ld_prm, n_prm[0])
            dve.wait_ge(ld_modT, 64)
            for s in range(2):
                m = V.scalar_tensor_tensor(mul1[:, s, :], modT[:, 1, s, :], 1.0, n1T, ALU.add, ALU.mult)
                if s:
                    m.then_inc(mul1_ready, 1)
                else:
                    link(m)
            dve.wait_ge(mul1_ready, 1)
            for t in range(NT):
                r, s = rows(t), stream(t)
                dve.wait_ge(x_tr, 2 * t + 1)
                for k in range(4):
                    m = V.tensor_scalar(hT[:, k, t * P:t * P + r], ps[:, 2 + 2 * (t % 2), k * P:k * P + r], mul1[:, s, k:k + 1],
                                        modT[:, 0, s, k:k + 1], ALU.mult, ALU.add)
                m.then_inc(x_evd, 1)
            V.scalar_tensor_tensor(lt1, lam, -1.0, lam, ALU.mult, ALU.max).then_inc(lam_abs, 1)

            def log1p(y, w, p):
                link(V.tensor_scalar(w, y, 2.0, None, ALU.add))
                link(V.reciprocal(w, w))
                link(V.tensor_tensor(y, y, w, ALU.mult))
                link(V.tensor_tensor(w, y, y, ALU.mult))
                link(V.tensor_scalar(p, w, LOG1P[-1], None, ALU.mult))
                for c in reversed(LOG1P[:-1]):
                    link(V.scalar_tensor_tensor(p, p, c, w, ALU.add, ALU.mult))
                link(V.scalar_tensor_tensor(p, p, 1.0, y, ALU.add, ALU.mult))
                link(V.tensor_scalar(p, p, 2.0, None, ALU.mult))

            dve.wait_ge(lam_exp, 1)
            log1p(lt1, lt2, c8)
            link(V.tensor_scalar(lt1, lam, -1.0, 0.0, ALU.mult, ALU.max))
            link(V.tensor_tensor(c8, c8, lt1, ALU.add))
            link(V.tensor_scalar(c8, c8, LRU_C, None, ALU.mult))
            link(V.tensor_scalar(nc8, c8, -1.0, None, ALU.mult))
            link(V.tensor_scalar(nbr, nbr, -1.0, None, ALU.mult))
            link(V.tensor_scalar(nbi, nbi, -1.0, None, ALU.mult))
            for b in range(4, 12):
                dve.wait_ge(ada_mm, b + 1)
                dve.wait_ge(mod_st[b % 2], 16 * (b // 2))
                V.tensor_copy(modrow[:, b % 2, :], ps[0:2, b % 2, :]).then_inc(mod_ev, 1)
            dve.wait_ge(x_tr, 2 * NT)
            for i in range(2):
                link(V.memset(xpad[i][:, 0:PAD], 0.0))
                link(V.memset(ga[i][:, SEQ:SEQ + PAD], 0.0))
            V.tensor_scalar(binq, binT[:, 8:12], DK ** -0.5, None, ALU.mult).then_inc(c8_ready, 1)

            def conv(f):
                x, u = xpad[f % 2], uu[f % 2][:, 0:UL]
                link(V.tensor_copy(x[:, PAD + SEQ:2 * PAD + SEQ], cv0[:, f, :]))
                dve.wait_ge(z_ev, 3 * (zblocks.index(f"xa{f}") + 1))
                link(V.tensor_scalar(u, x[:, 0:UL], convw[:, 0, f:f + 1], convb[:, f:f + 1], ALU.mult, ALU.add))
                for k in range(1, CONV_W):
                    link(V.scalar_tensor_tensor(u, x[:, k:k + UL], convw[:, k, f:f + 1], u, ALU.mult, ALU.add))
                link(V.tensor_copy(cvn[:, 0, f, :], x[:, SEQ:SEQ + PAD]))
                V.tensor_copy(cvn[:, 1, f, :], x[:, UL:XL]).then_inc(conv_done, 1)

            def gate_values(f):
                r, i, u = rr[:, 0:UL], ii[:, 0:UL], uu[f % 2][:, 0:UL]
                dve.wait_ge(lg_ev, 6 * f + 3)
                link(V.tensor_scalar(r, r, 1.0, None, ALU.add))
                V.reciprocal(r, r).then_inc(rg_ready, 1)
                dve.wait_ge(lg_ev, 6 * f + 6)
                link(V.tensor_scalar(i, i, 1.0, None, ALU.add))
                link(V.reciprocal(i, i))
                link(V.tensor_tensor(i, i, u, ALU.mult))

            def inner(f):
                th, d, p, g = rr[:, 0:UL], dd[:, 0:UL], pp[:, 0:UL], ga[f % 2][:, 0:UL]
                dve.wait_ge(z_ev, 3 * (zblocks.index(f"ga{f}") + 1))
                link(V.tensor_tensor(p, g, g, ALU.mult))
                link(V.tensor_scalar(p, p, GELU_C, 1.0, ALU.mult, ALU.add))
                link(V.tensor_tensor(p, p, g, ALU.mult))
                link(V.tensor_scalar(p, p, EXP_MAX / -GELU_S, None, ALU.max))
                dve.wait_ge(lru_ac, f + 1)
                link(V.tensor_scalar(d, th, 1.0, None, ALU.add))
                link(V.reciprocal(d, d))
                V.scalar_tensor_tensor(d, th, 2.0, d, ALU.mult, ALU.mult).then_inc(lru_d3, 1)

            def outer(f):
                i, a, d, p, u, g = ii[:, 0:UL], aa[:, 0:UL], dd[:, 0:UL], pp[:, 0:UL], uu[f % 2][:, 0:UL], ga[f % 2][:, 0:UL]
                s0 = SEQ + PAD
                dve.wait_ge(lru_d4a, 2 * f + 1)
                link(V.tensor_scalar(p, p, 1.0, None, ALU.add))
                link(V.reciprocal(p, p))
                link(V.tensor_tensor(p, p, g, ALU.mult))
                dve.wait_ge(lru_d4a, 2 * f + 2)
                V.tensor_tensor(i, i, d, ALU.mult).then_inc(lru_bx, 1)
                dve.wait_ge(lru_bx, f + 1)
                link(V.tensor_tensor_scan(u[:, 0:SEQ], a[:, 0:SEQ], i[:, 0:SEQ], 0.0, ALU.mult, ALU.add))
                V.tensor_tensor_scan(u[:, s0:UL], a[:, s0:UL], i[:, s0:UL], h0T[:, f:f + 1], ALU.mult, ALU.add).then_inc(lru_scan, 1)
                dve.wait_ge(lru_scan, f + 1)
                link(V.tensor_copy(hl[:, 0, f:f + 1], u[:, SEQ - 1:SEQ]))
                link(V.tensor_copy(hl[:, 1, f:f + 1], u[:, UL - 1:UL]))
                V.tensor_tensor(yT[:, f, 0:SEQ], u[:, 0:SEQ], p[:, 0:SEQ], ALU.mult).then_inc(lru_y, 1)
                V.tensor_tensor(yT[:, f, SEQ:T], u[:, s0:UL], p[:, s0:UL], ALU.mult).then_inc(lru_y, 1)
                dve.wait_ge(lru_y, 2 * f + 2)

            dve.wait_ge(c8_ready, 1)
            for i in range(2):
                dve.wait_ge(mod_st[i], 96)
            conv(0)
            for f in range(FT):
                gate_values(f)
                if f + 1 < FT:
                    conv(f + 1)
                inner(f)
                outer(f)
            dve.wait_ge(f_ld, 16)
            dve.wait_ge(z_mm, 48)
            V.scalar_tensor_tensor(wst, fro, -1.0, fro, ALU.mult, ALU.max).then_inc(f_abs, 1)
            dve.wait_ge(f_exp, 1)
            log1p(nmr, wkr, wst)
            link(V.scalar_tensor_tensor(fro, fro, 0.0, wst, ALU.min, ALU.subtract))
            for t in range(NT):
                c = slice(t * P, t * P + rows(t))
                link(V.tensor_tensor_scan(wst[:, c], ones[0:H_B, 0:rows(t)], fro[:, c], 0.0, ALU.mult, ALU.add))
            link(V.tensor_tensor(aro, zif[0:H_B, :], wst, ALU.subtract))
            link(V.memset(mprev[0:H_B, 0:1], 0.0))
            for t in range(NT):
                c, e = slice(t * P, t * P + rows(t)), t * P + rows(t)
                link(V.tensor_tensor_scan(mro[:, c], aro[:, c], aro[:, c], mprev[0:H_B, t:t + 1], ALU.max, ALU.max))
                nxt = mprev[0:H_B, t + 1:t + 2] if t < NT - 2 else mend[0:H_B, stream(t):stream(t) + 1]
                link(V.tensor_tensor(nxt, wst[:, e - 1:e], mro[:, e - 1:e], ALU.add))
                link(V.tensor_copy(mlast[0:H_B, t:t + 1], mro[:, e - 1:e]))
            link(V.scalar_tensor_tensor(nmr, wst, -1.0, mro, ALU.mult, ALU.subtract))
            for t in range(NT):
                c = slice(t * P, t * P + rows(t))
                link(V.tensor_scalar(wst[:, c], mro[:, c], mprev[0:H_B, t:t + 1], -1.0, ALU.subtract, ALU.mult))
                link(V.tensor_scalar(wkr[:, c], aro[:, c], mlast[0:H_B, t:t + 1], None, ALU.subtract))
            V.tensor_tensor(wcr[0:H_B], mprev[0:H_B], mlast[0:H_B], ALU.subtract).then_inc(row_ready, 1)
            for t in range(NT):
                r = rows(t)
                dve.wait_ge(z_ev, 51 + 2 * (t + 1))
                link(V.memset(vext[0:r, t, :, DK:DK + 1], 1.0))
                link(V.tensor_scalar(og[0:r, t, :], og[0:r, t, :], 1.0, None, ALU.add))
                link(V.reciprocal(og[0:r, t, :], og[0:r, t, :]))
                link(V.tensor_tensor(og[0:r, t, :], og[0:r, t, :], nwb[0:r, :], ALU.mult))
                if t == 6:
                    dve.wait_ge(f_exp, 2)
                    V.tensor_tensor(wcd[0:H_B], seleye[:, :, 0].unsqueeze(1).broadcast_to([H_B, NT, H_B]),
                                    wcr[0:H_B].unsqueeze(2).broadcast_to([H_B, NT, H_B]), ALU.mult).then_inc(row_exp, 1)
            dve.wait_ge(row_tr, 1)
            link(V.memset(cst[:, 0, :, :], 0.0))
            link(V.tensor_copy(wcb, ps[:, 4, 128:164].rearrange("p (c h) -> p c h", c=NT)))
            V.tensor_copy(colT[:, 0:NT - 1], ps[:, 4, 0:12 * (NT - 1)].rearrange("p (t a h) -> p t a h", a=3, h=H_B)).then_inc(col_ready, 1)
            V.tensor_copy(colT[0:DEC, NT - 1], ps[0:DEC, 4, 12 * (NT - 1):12 * NT].rearrange("p (a h) -> p a h", a=3)).then_inc(col_ready, 1)
            dve.wait_ge(col_ready, 2)

            def front(t):
                r, c = rows(t), slice(t * P, t * P + rows(t))
                if t >= 2:
                    dve.wait_ge(d_mm, t - 1)
                V.scalar_tensor_tensor(negm[:, t % 2, :, 0:r], mro[:, c].unsqueeze(1).broadcast_to([H_B, H_B, r]), -1.0,
                                       seleye[:, :, 0:r], ALU.mult, ALU.mult).then_inc(negm_ready, 1)
                dve.wait_ge(k_tr, t + 1)
                if t >= 1:
                    dve.wait_ge(c_mm, t)
                V.tensor_tensor(kw[0:r], ps[0:r, 0, :].rearrange("p (h d) -> p h d", h=H_B),
                                colT[0:r, t, 2, :].unsqueeze(2).broadcast_to([r, H_B, P]), ALU.mult).then_inc(kw_ready, 1)
                dve.wait_ge(s_mm, t + 1)
                dve.wait_ge(d_exp, t + 1)
                if t >= 2:
                    dve.wait_ge(n_mm, t - 1)
                V.tensor_tensor(prob[t % 2][0:r, :, 0:r], ps[0:r, 0, :].rearrange("p (h t) -> p h t", h=H_B)[:, :, 0:r],
                                decay[t % 2][0:r, :, 0:r], ALU.mult).then_inc(p_ready, 1)

            def carry(t):
                src, dst = (t % 2, (t + 1) % 2) if t < NT - 1 else (2, 3)
                dve.wait_ge(c_mm, t + 1)
                if 1 <= t < NT - 1:
                    dve.wait_ge(i_mm, t)
                if t == NT - 1:
                    dve.wait_ge(st_ld, 32)
                for h in range(H_B):
                    m = V.scalar_tensor_tensor(cst[:, dst, h, :], cst[:, src, h, :], wcb[:, t, h:h + 1],
                                               ps[:, 6 + h // 2, (h % 2) * 129:(h % 2) * 129 + 129], ALU.mult, ALU.add)
                    if h < H_B - 1:
                        link(m)
                    else:
                        m.then_inc(c_upd, 1)
                        dve.wait_ge(c_upd, t + 1)

            def back(t):
                r = rows(t)
                n = nd[t % 2]
                dve.wait_ge(n_ev, t + 1)
                dve.wait_ge(i_mm, t + 1)
                for h in range(H_B):
                    m = V.scalar_tensor_tensor(n[0:r, h, :], ps[0:r, 4 + h // 2, (h % 2) * 129:(h % 2) * 129 + 129],
                                               colT[0:r, t, 0, h:h + 1], n[0:r, h, :], ALU.mult, ALU.add)
                    if h < H_B - 1:
                        link(m)
                    else:
                        m.then_inc(nd_done, 1)
                        dve.wait_ge(nd_done, t + 1)
                link(V.scalar_tensor_tensor(den[0:r], n[0:r, :, DK], -1.0, n[0:r, :, DK], ALU.mult, ALU.max))
                link(V.tensor_tensor(den[0:r], den[0:r], colT[0:r, t, 1, :], ALU.max))
                link(V.reciprocal(rden[0:r], den[0:r]))
                V.tensor_tensor(hh[0:r, t, :].rearrange("p (h e) -> p h e", h=H_B), n[0:r, :, 0:DK],
                                rden[0:r].unsqueeze(2).broadcast_to([r, H_B, DK]), ALU.mult).then_inc(h_ready, 1)
                dve.wait_ge(h_ready, t + 1)

            front(0)
            for t in range(NT):
                if t + 1 < NT:
                    front(t + 1)
                carry(t)
                back(t)
            dve.wait_ge(h_sq, 4 * NT)
            V.tensor_scalar(ssqh, ssqh, 1.0 / DK, EPS, ALU.mult, ALU.add).then_inc(h_rt, 1)
            dve.wait_ge(h_rt, 2)
            link(V.reciprocal(rsth, ssqh))
            for t in range(NT):
                r = rows(t)
                for h in range(H_B):
                    m = V.scalar_tensor_tensor(og[0:r, t, h * P:(h + 1) * P], hh[0:r, t, h * P:(h + 1) * P],
                                               rsth[0:r, 4 * t + h:4 * t + h + 1], og[0:r, t, h * P:(h + 1) * P], ALU.mult, ALU.mult)
                    if h < H_B - 1:
                        link(m)
                m.then_inc(y_ready, 1)
            dve.wait_ge(bc_ld, 16 * 7)
            for s in range(2):
                n = P if s == 0 else DEC
                m = V.scalar_tensor_tensor(a2b[0:n, s, :], a2b[0:n, s, :], 1.0, n2b[0:n, :], ALU.add, ALU.mult)
                link(m)

            for t in range(NT):
                r, s = rows(t), stream(t)
                x = xr[0:r, t % 4, :]
                dve.wait_ge(o_mm, t + 1)
                dve.wait_ge(xr_ld[t % 4], 16 * (t // 4 + 1))
                o = ps[0:r, 2 * (t % 2):2 * (t % 2) + 2, :].rearrange("p b n -> p (b n)")
                link(V.tensor_tensor(h2[0:r, t, :], o, g1b[0:r, s, :], ALU.mult))
                V.tensor_tensor(x, x, h2[0:r, t, :], ALU.add).then_inc(x1_ready, 1)
                dve.wait_ge(x1_sq, t + 1)
                V.tensor_scalar(rstd2[0:r, t:t + 1], ssq2[0:r, t:t + 1], 1.0 / D, EPS, ALU.mult, ALU.add).then_inc(x1_rt, 1)
                dve.wait_ge(x1_rt, 2 * t + 2)
                link(V.reciprocal(rstd2[0:r, t:t + 1], rstd2[0:r, t:t + 1]))
                link(V.scalar_tensor_tensor(h2[0:r, t, :], x, rstd2[0:r, t:t + 1], a2b[0:r, s, :], ALU.mult, ALU.mult))
                V.tensor_tensor(h2[0:r, t, :], h2[0:r, t, :], sh2b[0:r, s, :], ALU.add).then_inc(h2_ready, 1)
            dve.wait_ge(h2_ready, NT)
            dve.wait_ge(x1_sq, NT)
            for s in range(4):
                dve.wait_ge(x1_st[s], 16 * (3 if s == 0 else 2))
            link(V.memset(acc, 0.0))
            link(V.memset(epsc, EPS))
            dve.sem_inc(u_free, 8)
            dve.sem_inc(r_cp, 1)
            dve.sem_inc(p_in, 1)
            dve.wait_ge(o_mm, NT)
            link(V.memset(ps[0:DEC, 0:2, :], 0.0))
            for g in range(GROUPS):
                q = slice(g * DEC, (g + 1) * DEC)
                link(V.tensor_copy(sel32[q], ident[0:DEC, 0:DEC]))
                if g:
                    link(V.tensor_copy(h2[q, NT - 1, :], h2[0:DEC, NT - 1, :]))
            link(V.memset(frs, 1.0))
            rc, mc, fc = Chain(dve, route_step), Chain(dve, mix_step), Chain(dve, fin_step)

            def hold():
                dve.sem_inc(dve_turn, 1)

            def top8(out, idx, src, rest):
                V.max_index(idx, out, src)
                return V.match_replace(rest, out, src, NEG_MAX)

            def route(t, m, r):
                rc.base, rc.n = m * K_ROUTE, 0
                s2 = [slice(c * P, (c + 1) * P) for c in range(2)]
                lo = [slice(c * TOPK, c * TOPK + 8) for c in range(2)]
                hi = [slice(c * TOPK + 8, c * TOPK + 16) for c in range(2)]
                sc = ps[0:r, 5, 0:256]
                dve.wait_ge(r_mm, m + 2)
                hold()
                V.max(top[0:r, lo[0]], sc[:, s2[0]])
                rc.link(V.max(top[0:r, lo[1]], sc[:, s2[1]]))
                hold()
                for c in range(2):
                    last = top8(top[0:r, lo[c]], topi[0:r, lo[c]], sc[:, s2[c]], swk[0:r, s2[c]])
                rc.link(last)
                hold()
                V.max(top[0:r, hi[0]], swk[0:r, s2[0]])
                rc.link(V.max(top[0:r, hi[1]], swk[0:r, s2[1]]))
                hold()
                for c in range(2):
                    V.max_index(topi[0:r, hi[c]], top[0:r, hi[c]], swk[0:r, s2[c]])
                rc.link(V.tensor_tensor(cand[0:r].rearrange("p (a b) -> p a b", a=TOPK),
                                        top[0:r, 0:TOPK].unsqueeze(2).broadcast_to([r, TOPK, TOPK]),
                                        top[0:r, TOPK:2 * TOPK].unsqueeze(1).broadcast_to([r, TOPK, TOPK]), ALU.add))
                hold()
                V.max(sv[0:r, 0:8], cand[0:r])
                dve.wait_ge(q_rt, m + 1)
                V.reciprocal(qrs[0:r], qrt[0:r]).then_inc(r_cp, 1)
                rc.link(V.tensor_copy(topf[0:r], topi[0:r]))
                hold()
                rc.link(top8(sv[0:r, 0:8], si[0:r, 0:8], cand[0:r], cand2[0:r]))
                hold()
                V.tensor_scalar(nsv0[0:r], sv[0:r, 0:1], -1.0, qrs[0:r], ALU.mult, ALU.mult)
                rc.link(V.max(sv[0:r, 8:16], cand2[0:r]))
                hold()
                V.max_index(si[0:r, 8:16], sv[0:r, 8:16], cand2[0:r]).then_inc(p_in, 1)
                dve.wait_ge(p_in, m + 2)
                V.tensor_scalar(sab[0:r, 0:TOPK], si[0:r], 4, None, ALU.logical_shift_right)
                rc.link(V.tensor_scalar(sab[0:r, TOPK:2 * TOPK], si[0:r], 15, None, ALU.bitwise_and))
                rc.link(V.tensor_copy(sabf[0:r], sab[0:r]))
                half = [slice(c * TOPK, (c + 1) * TOPK) for c in range(2)]
                for c in range(2):
                    last = V.tensor_tensor(hot[c][0:r], sabf[0:r, half[c]].unsqueeze(2).broadcast_to([r, TOPK, TOPK]),
                                           pos16[0:r].unsqueeze(1).broadcast_to([r, TOPK, TOPK]), ALU.is_equal)
                rc.link(last)
                for c in range(2):
                    last = V.tensor_tensor(hot[c][0:r], hot[c][0:r],
                                           topf[0:r, half[c]].unsqueeze(1).broadcast_to([r, TOPK, TOPK]), ALU.mult)
                rc.link(last)
                for c in range(2):
                    last = V.tensor_reduce(e12[0:r, half[c]], hot[c][0:r], AXX, ALU.add)
                rc.link(last)
                parts = [(slice(0, P), 0, TOPK)] if r == P else [
                    (slice(g * DEC, (g + 1) * DEC), g * TOPK_S, TOPK_S) for g in range(GROUPS)]
                for q, c, k in parts:
                    last = V.scalar_tensor_tensor(gidx_t[q, t, 0:k], e12[0:r, c:c + k], float(P), e12[0:r, TOPK + c:TOPK + c + k],
                                                  ALU.mult, ALU.add)
                last.then_inc(idx_ready, 1)
                dve.wait_ge(p_exp, m + 1)
                rc.link(V.reciprocal(prs[0:r], psm[0:r]))
                for q, c, k in parts:
                    last = V.tensor_scalar(gate_t[q, t, 0:k], pexp[0:r, c:c + k], prs[0:r], None, ALU.mult)
                rc.link(last)
                assert rc.n == K_ROUTE, rc.n
                hold()

            def dot_products(h, t, k):
                for j in range(k):
                    dve.wait_ge(u_ld[j % 8], landed(h, t, j))
                    dve.wait_ge(u_free, slot0(h, t) + (j + 7))
                    V.scalar_tensor_tensor(udump[j % 2], uring[:, j % 8, :], 1.0, h2[:, t, :], ALU.mult, ALU.mult,
                                           accum_out=dots[:, j:j + 1]).then_inc(u_free, 1)
                dve.wait_ge(u_free, slot0(h, t) + (k + 8))

            def expert_weights(h, t, k):
                n = number(h, t)
                mc.base, mc.n = n * K_MIX, 0
                d, g, e = dots[:, 0:k], gl[:, 0:k], gl2[:, 0:k]
                mc.link(V.tensor_tensor(g, d, d, ALU.mult))
                mc.link(V.tensor_scalar(g, g, GELU_C, 1.0, ALU.mult, ALU.add))
                mc.link(V.tensor_tensor(g, g, d, ALU.mult))
                V.tensor_scalar(g, g, EXP_MAX / -GELU_S, None, ALU.max).then_inc(g_in, 1)
                dve.wait_ge(g_exp, n + 1)
                mc.link(V.tensor_scalar(e, e, 1.0, None, ALU.add))
                mc.link(V.reciprocal(e, e))
                mc.link(V.tensor_tensor(e, e, d, ALU.mult))
                V.tensor_tensor(wgt[:, 0:k], e, gate_t[:, t, 0:k], ALU.mult).then_inc(w_ready, 1)
                dve.wait_ge(w_ready, n + 1)
                assert mc.n == K_MIX, mc.n
                hold()

            def accumulate(before, n, t, r):
                dve.wait_ge(v_free, before + 8)
                V.tensor_tensor(acc[0:r, t, :], acc[0:r, t, :], ps[0:r, 0:2, :].rearrange("p b n -> p (b n)"),
                                ALU.add).then_inc(acc_done, 1)
                dve.wait_ge(acc_done, n + 1)

            def final(t, r):
                fc.base, fc.n = t * K_FIN, 0
                a = feat(acc[0:r, t, :])
                if r == DEC:
                    dve.wait_ge(g2_ld, 48)
                else:
                    dve.wait_ge(g2_ld, 32)
                fc.link(V.tensor_tensor(a, a, g2b if r == P else g2s, ALU.mult))
                dve.wait_ge(x1_ld, t * 16 + 16)
                fc.link(V.tensor_tensor(a, a, x1s[0:r], ALU.add))
                fc.link(V.scalar_tensor_tensor(fdump[0:r], a, 1.0, a, ALU.mult, ALU.mult, accum_out=fss[0:r]))
                V.tensor_scalar(frs[0:r], fss[0:r], 1.0 / D, EPS, ALU.mult, ALU.add).then_inc(f_var, 1)
                dve.wait_ge(f_rt, t + 1)
                fc.link(V.reciprocal(frs[0:r], frs[0:r]))
                V.scalar_tensor_tensor(a, a, frs[0:r], fwb[0:r], ALU.mult, ALU.mult).then_inc(y_out, 1)
                assert fc.n == K_FIN, fc.n

            route(0, 0, P)
            route(1, 1, P)

            def step(h, t, r, tp, rp, ta, ra, last):
                k = slots(r)
                dot_products(h, t, k)
                accumulate(slot0(h, t), number(h, t), tp, rp)
                expert_weights(h, t, k)
                if ta is not None:
                    route(ta, number(h, t) + 2, ra)
                if last and not first(t):
                    final(tp, rp)

            each_step(dve, step)
            accumulate(HEADS * SLOTS, HEADS * NT, NT - 1, DEC)
            final(NT - 1, DEC)


def kernel(**inputs):
    import numpy as _np
    import concourse.bacc as _bacc
    from concourse.bass_utils import run_bass_kernel_spmd as _run

    nc = _bacc.Bacc("TRN2", target_bir_lowering=False, num_devices=1)
    arrays, A = {}, {}
    for name, a in inputs.items():
        a = _np.ascontiguousarray(a)
        arrays[f"in_{name}"] = a
        A[name] = nc.dram_tensor(f"in_{name}", a.shape, mybir.dt.from_np(a.dtype), kind="ExternalInput").ap()
    outs = [nc.dram_tensor(f"out_{i}", s, F32, kind="ExternalOutput").ap() for i, s in enumerate(OUTS)]
    build(nc, A, outs)
    r = _run(nc, [arrays], core_ids=[0])
    return tuple(r.results[0][f"out_{i}"] for i in range(len(OUTS)))
```
